# Optimizing a Trainium2 kernel written in Bass

```python
import math
import jax, jax.numpy as jnp
from jax import lax
import numpy as np

D_MODEL = 1024
BATCH = 1
SEQ = 1024
DEPTH = 2

N_A_LAYERS = DEPTH // 2
N_B_LAYERS = DEPTH - N_A_LAYERS
M_HEADS = 4
M_V_DIM = D_MODEL // M_HEADS
M_QK_DIM = M_V_DIM // 2
M_CHUNK = 128
GATE_CAP = 15.0
M_IN_DIM = 2 * M_HEADS * M_QK_DIM + 2 * D_MODEL + 2 * M_HEADS
A_HEADS = 16
A_KV_HEADS = 4
A_GROUP = A_HEADS // A_KV_HEADS
A_HEAD_DIM = 64
WINDOW = 128
ROPE_DIM = A_HEAD_DIM // 4
ROPE_THETA = 500000.0
D_FF = 4 * D_MODEL
DEEPNORM_ALPHA = (2 * DEPTH) ** 0.25
DEEPNORM_BETA = (8 * DEPTH) ** -0.25
LN_EPS = 1e-5
RMS_EPS = 1e-6
N_MOD = 6

kernel_name = "yoco_mlstm_swa_sink_hybrid"

F32 = jnp.float32

def layer_norm(x, g, b):
    xf = x.astype(F32)
    mu = jnp.mean(xf, axis=-1, keepdims=True)
    var = jnp.mean(jnp.square(xf - mu), axis=-1, keepdims=True)
    y = (xf - mu) * lax.rsqrt(var + LN_EPS)
    return (y * g.astype(F32) + b.astype(F32)).astype(x.dtype)

def modulate(x, shift, scale):
    return x * (1 + scale) + shift

def rope_partial(x, pos):
    half = ROPE_DIM // 2
    inv_freq = ROPE_THETA ** (-jnp.arange(half, dtype=F32) / half)
    ang = pos.astype(F32)[..., None] * inv_freq
    cos = jnp.cos(ang)[:, :, None, :]
    sin = jnp.sin(ang)[:, :, None, :]
    xr = x[..., :ROPE_DIM].astype(F32)
    x1, x2 = xr[..., :half], xr[..., half:]
    rot = jnp.concatenate([x1 * cos - x2 * sin, x2 * cos + x1 * sin], axis=-1).astype(x.dtype)
    return jnp.concatenate([rot, x[..., ROPE_DIM:]], axis=-1)

def mlstm_mixer(u, w_in, b_gates, norm_w, w_out):
    B, S, _ = u.shape
    H, L, dk, dv = M_HEADS, M_CHUNK, M_QK_DIM, M_V_DIM
    nq = H * dk
    proj = u @ w_in
    q, k, v, o, gi, gf = jnp.split(
        proj, [nq, 2 * nq, 2 * nq + D_MODEL, 2 * nq + 2 * D_MODEL, 2 * nq + 2 * D_MODEL + H], axis=-1)
    gates = (jnp.concatenate([gi, gf], axis=-1) + b_gates).astype(F32)
    gates = GATE_CAP * jnp.tanh(gates / GATE_CAP)
    log_i = gates[..., :H]
    log_f = jax.nn.log_sigmoid(gates[..., H:])
    nc = S // L

    def to_chunks(t, d):
        return t.astype(F32).reshape(B, nc, L, H, d).transpose(1, 0, 3, 2, 4)

    def gate_chunks(t):
        return t.reshape(B, nc, L, H).transpose(1, 0, 3, 2)

    qc = to_chunks(q, dk)
    kc = to_chunks(k, dk) / math.sqrt(dk)
    vc = to_chunks(v, dv)
    lic, lfc = gate_chunks(log_i), gate_chunks(log_f)
    causal = jnp.tril(jnp.ones((L, L), dtype=bool))

    def step(carry, inp):
        C, n, m = carry
        qb, kb, vb, li, lf = inp
        bcum = jnp.cumsum(lf, axis=-1)
        dmat = bcum[..., :, None] - bcum[..., None, :] + li[..., None, :]
        dmat = jnp.where(causal, dmat, -jnp.inf)
        inter = bcum + m[..., None]
        m_t = jnp.maximum(inter, jnp.max(dmat, axis=-1))
        w_intra = jnp.exp(dmat - m_t[..., None])
        w_inter = jnp.exp(inter - m_t)
        s_qk = jnp.einsum('bhtd,bhsd->bhts', qb, kb) * w_intra
        num = (w_inter[..., None] * jnp.einsum('bhvd,bhtd->bhtv', C, qb)
               + jnp.einsum('bhts,bhsv->bhtv', s_qk, vb))
        den = w_inter * jnp.einsum('bhd,bhtd->bht', n, qb) + jnp.sum(s_qk, axis=-1)
        h = num / jnp.maximum(jnp.abs(den), jnp.exp(-m_t))[..., None]
        b_last = bcum[..., -1]
        d_end = b_last[..., None] - bcum + li
        m_new = jnp.maximum(b_last + m, jnp.max(d_end, axis=-1))
        w_state = jnp.exp(d_end - m_new[..., None])
        decay = jnp.exp(b_last + m - m_new)
        C_new = decay[..., None, None] * C + jnp.einsum('bhs,bhsv,bhsd->bhvd', w_state, vb, kb)
        n_new = decay[..., None] * n + jnp.einsum('bhs,bhsd->bhd', w_state, kb)
        return (C_new, n_new, m_new), h

    init = (jnp.zeros((B, H, dv, dk), F32), jnp.zeros((B, H, dk), F32), jnp.zeros((B, H), F32))
    _, hs = lax.scan(step, init, (qc, kc, vc, lic, lfc))
    hs = hs * lax.rsqrt(jnp.mean(jnp.square(hs), axis=-1, keepdims=True) + RMS_EPS)
    hs = hs.transpose(1, 0, 3, 2, 4).reshape(B, S, H * dv)
    hs = hs * norm_w.astype(F32) * jax.nn.sigmoid(o.astype(F32))
    return hs.astype(u.dtype) @ w_out

def swa_sink_attention(q, k, v, sinks):
    B, S = q.shape[:2]
    L = WINDOW
    nb = S // L
    qb = q.reshape(B, nb, L, A_KV_HEADS, A_GROUP, A_HEAD_DIM)

    def band(t):
        tb = t.reshape(B, nb, L, A_KV_HEADS, A_HEAD_DIM)
        prev = jnp.pad(tb[:, :-1], ((0, 0), (1, 0), (0, 0), (0, 0), (0, 0)))
        return jnp.concatenate([prev, tb], axis=2)

    kb, vb = band(k), band(v)
    scores = jnp.einsum('bnqkgd,bnskd->bnkgqs', qb, kb).astype(F32) / math.sqrt(A_HEAD_DIM)
    qi = jnp.arange(L)[:, None]
    sj = jnp.arange(2 * L)[None, :]
    in_window = (sj > qi) & (sj <= qi + L)
    blk = jnp.arange(nb)[:, None, None]
    mask = in_window[None] & ((blk > 0) | (sj[None] >= L))
    scores = jnp.where(mask[None, :, None, None], scores, -jnp.inf)
    sink = sinks.astype(F32).reshape(A_KV_HEADS, A_GROUP)[None, None, :, :, None, None]
    mx = jnp.maximum(jnp.max(scores, axis=-1, keepdims=True), sink)
    e = jnp.exp(scores - mx)
    probs = e / (jnp.sum(e, axis=-1, keepdims=True) + jnp.exp(sink - mx))
    out = jnp.einsum('bnkgqs,bnskd->bnqkgd', probs.astype(v.dtype), vb)
    return out.reshape(B, S, A_HEADS * A_HEAD_DIM)

def setup_inputs(seed: int = 0) -> dict:
    key = jax.random.key(seed)
    ks = jax.random.split(key, 24)
    nrm = jax.random.normal
    D = D_MODEL
    kv_dim = A_KV_HEADS * A_HEAD_DIM
    x = nrm(ks[0], (BATCH, SEQ, D), F32)
    c = nrm(ks[1], (BATCH, D), F32)
    offsets = jax.random.randint(ks[2], (BATCH, 1), 0, 1024, dtype=jnp.int32)
    positions = offsets + jnp.arange(SEQ, dtype=jnp.int32)[None, :]
    ada_w = nrm(ks[3], (DEPTH, D, N_MOD * D), F32) * (0.1 * D ** -0.5)
    ada_b = nrm(ks[4], (DEPTH, N_MOD * D), F32) * 0.01
    kv_ada_w = nrm(ks[5], (D, 2 * D), F32) * (0.1 * D ** -0.5)
    kv_ada_b = nrm(ks[6], (2 * D,), F32) * 0.01
    a_w_in = nrm(ks[7], (N_A_LAYERS, D, M_IN_DIM), F32) * D ** -0.5
    b_i = nrm(ks[8], (N_A_LAYERS, M_HEADS), F32) * 0.01
    b_f = jnp.linspace(3.0, 6.0, M_HEADS, dtype=F32)[None, :] + nrm(ks[9], (N_A_LAYERS, M_HEADS), F32) * 0.01
    a_b_gates = jnp.concatenate([b_i, b_f], axis=-1)
    a_norm_w = 1.0 + 0.02 * nrm(ks[10], (N_A_LAYERS, D), F32)
    a_w_out = nrm(ks[11], (N_A_LAYERS, D, D), F32) * (D ** -0.5 * DEEPNORM_BETA)
    w_k = nrm(ks[12], (D, kv_dim), F32) * D ** -0.5
    w_v = nrm(ks[13], (D, kv_dim), F32) * (D ** -0.5 * DEEPNORM_BETA)
    w_kv = jnp.concatenate([w_k, w_v], axis=-1)
    b_w_q = nrm(ks[14], (N_B_LAYERS, D, A_HEADS * A_HEAD_DIM), F32) * D ** -0.5
    b_sinks = nrm(ks[15], (N_B_LAYERS, A_HEADS), F32) * 0.5
    b_w_o = nrm(ks[16], (N_B_LAYERS, A_HEADS * A_HEAD_DIM, D), F32) * ((A_HEADS * A_HEAD_DIM) ** -0.5 * DEEPNORM_BETA)
    mlp_w_up = nrm(ks[17], (DEPTH, D, D_FF), F32) * D ** -0.5
    mlp_w_down = nrm(ks[18], (DEPTH, D_FF, D), F32) * (D_FF ** -0.5 * DEEPNORM_BETA)
    ln_g = 1.0 + 0.02 * nrm(ks[19], (2 * DEPTH, D), F32)
    ln_b = 0.02 * nrm(ks[20], (2 * DEPTH, D), F32)
    return {"x": x, "c": c, "positions": positions, "ada_w": ada_w, "ada_b": ada_b,
            "kv_ada_w": kv_ada_w, "kv_ada_b": kv_ada_b, "a_w_in": a_w_in, "a_b_gates": a_b_gates,
            "a_norm_w": a_norm_w, "a_w_out": a_w_out, "w_kv": w_kv, "b_w_q": b_w_q,
            "b_sinks": b_sinks, "b_w_o": b_w_o, "mlp_w_up": mlp_w_up, "mlp_w_down": mlp_w_down,
            "ln_g": ln_g, "ln_b": ln_b}

def reference(x, c, positions, ada_w, ada_b, kv_ada_w, kv_ada_b, a_w_in, a_b_gates, a_norm_w,
              a_w_out, w_kv, b_w_q, b_sinks, b_w_o, mlp_w_up, mlp_w_down, ln_g, ln_b):
    B, S, _ = x.shape
    kv_dim = A_KV_HEADS * A_HEAD_DIM
    cs = jax.nn.silu(c)
    h = x
    k_sh = v_sh = None
    for layer in range(DEPTH):
        if layer == N_A_LAYERS:
            kv_mod = (cs @ kv_ada_w + kv_ada_b)[:, None, :]
            kv_shift, kv_scale = jnp.split(kv_mod, 2, axis=-1)
            kv = modulate(h, kv_shift, kv_scale) @ w_kv
            k_sh = rope_partial(kv[..., :kv_dim].reshape(B, S, A_KV_HEADS, A_HEAD_DIM), positions)
            v_sh = kv[..., kv_dim:].reshape(B, S, A_KV_HEADS, A_HEAD_DIM)
        mod = (cs @ ada_w[layer] + ada_b[layer])[:, None, :]
        sh_m, sc_m, g_m, sh_f, sc_f, g_f = jnp.split(mod, N_MOD, axis=-1)
        u = modulate(h, sh_m, sc_m)
        if layer < N_A_LAYERS:
            y = mlstm_mixer(u, a_w_in[layer], a_b_gates[layer], a_norm_w[layer], a_w_out[layer])
        else:
            j = layer - N_A_LAYERS
            q = rope_partial((u @ b_w_q[j]).reshape(B, S, A_HEADS, A_HEAD_DIM), positions)
            y = swa_sink_attention(q, k_sh, v_sh, b_sinks[j]) @ b_w_o[j]
        h = layer_norm(DEEPNORM_ALPHA * h + (1 + g_m) * y, ln_g[2 * layer], ln_b[2 * layer])
        u = modulate(h, sh_f, sc_f)
        y = jnp.square(jax.nn.relu(u @ mlp_w_up[layer])) @ mlp_w_down[layer]
        h = layer_norm(DEEPNORM_ALPHA * h + (1 + g_f) * y, ln_g[2 * layer + 1], ln_b[2 * layer + 1])
    return h


_drawn_inputs = setup_inputs


def setup_inputs(seed=0):
    import zlib

    import numpy as np

    out = dict(_drawn_inputs(seed))
    spreads = {}
    factors = {'ada_b': 4.497,
     'kv_ada_w': 4.989,
     'kv_ada_b': 30.505,
     'a_norm_w': 26.567,
     'b_sinks': 38.656}
    for name, (base, spread) in spreads.items():
        noise = np.random.default_rng([zlib.crc32(name.encode()), seed]).standard_normal(out[name].shape)
        drawn = base * np.exp(spread * noise) if base else spread * noise
        out[name] = __import__('jax').numpy.asarray(drawn.astype(out[name].dtype))
    for name, factor in factors.items():
        out[name] = (out[name] * factor).astype(out[name].dtype)
    return out
```

```python
import math
from contextlib import ExitStack

import numpy as np
import concourse.bass as bass
from concourse import mybir

F32 = mybir.dt.float32
F32R = mybir.dt.float32r
I32 = mybir.dt.int32
ALU = mybir.AluOpType
ACT = mybir.ActivationFunctionType

P = 128
S = 1024
D = 1024
DFF = 4 * D
T = S // P
K = D // P
HALF = 512
H = 4
DV = D // H
HC = H * T
AH = 16
UNITS = AH // 4 * T
HD = 64
GROUP = 4
ROT = HD // 4
RH = ROT // 2
THETA = 500000.0
CAP = 15.0
ALPHA = 4.0 ** 0.25
LN_EPS = 1e-5
RMS_EPS = 1e-6
MASKED = -3.0e38
ROUNDER = 1.5 * 2.0 ** 23
TWO_PI = (6.28125, 1.9350051879882812e-3, 3.0199159819733e-7)
PI_IN = 3.1415925

SC_M0, SH_M0, G_M0, SH_F0, SC_F0, G_F0, SH_KV, SC_KV, SH_M1, SC_M1, G_M1, SH_F1, SC_F1, G_F1 = range(14)
NVEC = 14

W_QK, W_V, W_O, W_OUT, W_MLP0 = 0, 8, 16, 24, 32
CHUNKS = DFF // HALF
W_KV = W_MLP0 + 8 * CHUNKS
W_Q = W_KV + 4
W_OP = W_Q + 8
W_MLP1 = W_OP + 8
N_W = W_MLP1 + 8 * CHUNKS

SLOTS = 6
RING = 3


def slot_of(w):
    for first in (W_MLP0, W_MLP1):
        if first <= w < first + 8 * CHUNKS:
            j = (w - first) % 8
            return j % 2 if j < 4 else j - 2
    if w < W_MLP0:
        return (w - W_MLP0) % SLOTS
    if w < W_OP:
        return (w - W_KV) % SLOTS
    return [0, 1, 2, 3, 2, 3, 4, 5][w - W_OP]


def former_in_slot(w):
    for first in (W_MLP0, W_MLP1):
        if first <= w < first + 8 * CHUNKS:
            j = (w - first) % 8
            if j >= 2 and (w >= first + 8 or j < 4):
                return w - (2 if j < 4 else 8)
            if w >= first + 8:
                return w - 6
    before = [x for x in range(w) if slot_of(x) == slot_of(w)]
    return before[-1] if before else None


def is_scaled(w):
    if W_OUT <= w < W_MLP0 or W_OP <= w < W_MLP1:
        return True
    return any(f <= w < f + 8 * CHUNKS and (w - f) % 8 >= 4 for f in (W_MLP0, W_MLP1))


CHUNK_LOADS = [4, 2, 5, 3, 6, 7, 8, 9]


def load_order():
    out = []

    def ada(v, ks=range(K)):
        out.extend(("ada", v, k) for k in ks)

    def w(*blocks):
        out.extend(("w", b) for b in blocks)

    ada(SC_M0), ada(SH_M0)
    w(0, 1, 2, 3, 4, 5, 6, 7, 8, 9, 10)
    ada(G_M0)
    w(11, 12, 13)
    for t in range(T):
        if t == T - 1:
            w(14, 15)
        ada((SH_F0, SC_F0)[t // 4], range(2 * (t % 4), 2 * (t % 4) + 2))
    for t in range(T):
        if t == T - 1:
            w(18, 17, 19)
        ada((G_F0, SH_KV)[t // 4], range(2 * (t % 4), 2 * (t % 4) + 2))
        if t == 1:
            w(16)
    w(20, 21, 22, 23, 24, 25, 26, 27, 28, 29, 30, 31, 32, 33)
    for c in range(CHUNKS):
        w(*[W_MLP0 + 8 * c + j for j in CHUNK_LOADS])
        if c < CHUNKS - 1:
            ada(SC_KV + c)
    w(98, 99, 100, 101, 102, 103, 104, 105, 106, 107, 108, 109, 110, 111, 114, 115, 112, 113, 116, 117)
    for c in range(CHUNKS):
        w(*[W_MLP1 + 8 * c + j for j in CHUNK_LOADS if W_MLP1 + 8 * c + j < N_W])
    return out


ORDER = load_order()
NUMBER = {x: n for n, x in enumerate(ORDER)}
LOADS_MLP0, LOADS_MLP1 = NUMBER["w", W_MLP0 + 4], NUMBER["w", W_MLP1 + 4]
N_LOADS = len(ORDER)
WEIGHTS_BEFORE = [sum(x[0] == "w" for x in ORDER[:n]) for n in range(N_LOADS + 1)]
SCALED_BEFORE = [sum(x[0] == "w" and is_scaled(x[1]) for x in ORDER[:n]) for n in range(N_LOADS + 1)]
assert sorted(x[1] for x in ORDER if x[0] == "w") == list(range(N_W))


def group_engines():
    out, first = "", {}

    def add(name, what):
        nonlocal out
        first[name] = len(out)
        out += what

    add("qk", "A" * 16)
    add("v", "D" * 16)
    add("o0", "A" * 8)
    add("o1a", "A" * 2)
    add("gm0", "A" * 2)
    add("o1b", "A" * 6)
    add("out0", "D" * 8)
    add("out1a", "D" * 4)
    add("gf0", "A" * 2)
    add("out1b", "D" * 4)
    add("mlp0", ("A" * 8 + "D" * 16) * CHUNKS)
    add("kva", "D" * 3)
    add("gm1", "A" * 2)
    add("kvb", "D" * 5)
    add("q", "D" * 16)
    add("op0", "D" * 8)
    add("op1a", "D" * 4)
    add("gf1", "A" * 2)
    add("op1b", "D" * 4)
    add("mlp1", ("A" * 8 + "D" * 16) * CHUNKS)
    return out, first


ENGINES, FIRST = group_engines()
ACT_BEFORE = [ENGINES[:g].count("A") for g in range(len(ENGINES) + 1)]
DVE_BEFORE = [ENGINES[:g].count("D") for g in range(len(ENGINES) + 1)]

def groups_through(w):
    for first, name in ((W_MLP0, "mlp0"), (W_MLP1, "mlp1")):
        if first <= w < first + 8 * CHUNKS:
            c, j = divmod(w - first, 8)
            return FIRST[name] + 24 * c + (2 * j + 2 if j < 4 else 24)
    if w < W_V:
        return FIRST["qk"] + 2 * w + 2
    for first, names in ((W_OP, ("op0", "op1b")), (W_Q, ("q", "q")), (W_KV, ("kvb", "kvb")), (W_OUT, ("out0", "out1b")),
                         (W_O, ("o0", "o1b")), (W_V, ("v", "v"))):
        if w >= first:
            second = (w - first) // 4
            size = {"q": T * (1 + second), "v": T * (1 + second), "kvb": 5, "o1b": 6, "out1b": 4, "op1b": 4}
            return FIRST[names[second]] + size.get(names[second], T)


TR_HS, TR_LN0, TR_KV, TR_Q, TR_LN2 = (T * i for i in range(5))


LAG = 2


def build(nc, stream, xt, x, consts, out):
    ctx = ExitStack()

    def sb(name, shape, dt=F32, where=ctx):
        return where.enter_context(nc.sbuf_tensor(name, shape, dt))

    def sem(name):
        return ctx.enter_context(nc.semaphore(name))

    with ctx:
        resid = sb("resid", [P, T, H * (DV + 1)])
        uhi = sb("uhi", [P, K, S], F32R)
        ulo = sb("ulo", [P, K, S], F32R)
        whi = sb("whi", [P, SLOTS, D], F32R)
        wlo = sb("wlo", [P, SLOTS, D], F32R)
        stage = sb("stage", [P, 2, D])
        scratch = sb("scratch", [P, 2, HALF])
        acc = sb("acc", [P, D])
        mods = sb("mods", [P, NVEC, K])
        mulv = sb("mulv", [P, 5, K])
        addv = sb("addv", [P, 5, K])
        fcols = sb("fcols", [P, 7, K])
        ident = sb("ident", [P, P])
        ones = sb("ones", [P, 1])
        cs = sb("cs", [P, 2, K])
        stats = sb("stats", [P, 2, 12])
        moments = sb("moments", [P, 2, 2])
        neghalf = sb("neghalf", [P, H])
        rstd = sb("rstd", [P, 2, 1])
        nmr = sb("nmr", [P, 2, 1])
        sumsq, factor, mean = stats[:, 1, 4:4 + H], stats[:, 1, 0:H], stats[:, 0, H:2 * H]

        with ExitStack() as a:
            cstate = sb("cstate", [P, H, DV + 1], where=a)
        gate_row = sb("gate_row", [P, H * (DV + 1)])
        with ExitStack() as a:
            negm = sb("negm", [HC, P], where=a)
            winter = sb("winter", [HC, P], where=a)
            cols = sb("cols", [P, 5, HC], where=a)
        with ExitStack() as a:
            rope = sb("rope", [P, T, 2 * ROT], where=a)
            angle = sb("angle", [P, T, RH], where=a)
            turns = sb("turns", [P, T, RH], where=a)
            sinks = sb("sinks", [P, AH], where=a)
            posi = sb("posi", [P, T], I32, where=a)
        small = sb("small", [P, 416])
        with ExitStack() as a:
            dmat = sb("dmat", [P, H, P], where=a)
            smat = sb("smat", [P, H, P], where=a)
            ktok = sb("ktok", [P, H, P], where=a)
            gw = sb("gw", [P, K * 8], where=a)
            gwhi = sb("gwhi", [P, K * 8], F32R, where=a)
            gwlo = sb("gwlo", [P, K * 8], F32R, where=a)
            gt = sb("gt", [P, 4, 2 * HC], where=a)
        m_prev_col = gt[0:HC, 3, 0:1]
        with ExitStack() as a:
            probst = sb("probst", [P, 2, 2, HALF], where=a)
        lnrows = sb("lnrows", [P, 2, D])
        with ExitStack() as a:
            qk = sb("qk", [P, T, D], where=a)
        with ExitStack() as a:
            hhi = sb("hhi", [P, 4, S], F32R, where=a)
            hlo = sb("hlo", [P, 4, S], F32R, where=a)
        with ExitStack() as a:
            kt = sb("kt", [P, 2, S], where=a)
            vv = sb("vv", [P, T, 4 * HD], where=a)
            probs = sb("probs", [P, 3, GROUP, 2 * P], where=a)
            mask = sb("mask", [P, 2 * P], where=a)
            rtmp = sb("rtmp", [P, 2, 8, ROT], where=a)
            att = sb("att", [P, 3, 6, GROUP], where=a)
        aux = sb("aux", [P, 8 * D])
        ps = ctx.enter_context(nc.psum_tensor("ps", [P, 8, HALF], F32))
        M = RING
        X = RING + 1
        resid_dram = nc.dram_tensor("resid_dram", (T, P, D), F32, kind="Internal").ap()

        stage_loaded = [sem("stage_loaded0"), sem("stage_loaded1")]
        loads_used = sem("loads_used")
        scaled = sem("scaled")
        hi_ready = sem("hi_ready")
        group_done = sem("group_done")
        act_evac = sem("act_evac")
        dve_evac = sem("dve_evac")
        consts_in = sem("consts_in")
        xt_in = sem("xt_in")
        dve_step = sem("dve_step")
        act_step = sem("act_step")
        pool_step = sem("pool_step")
        sum_done = sem("sum_done")
        sum_read = sem("sum_read")
        gate_m = sem("gate_m")
        u_made = sem("u_made")
        u_hi = sem("u_hi")
        u_ready = sem("u_ready")
        gate_e = sem("gate_e")
        gate_v = sem("gate_v")
        diag_ready = sem("diag_ready")
        gate_row_ready = sem("gate_row_ready")
        mix = sem("mix")
        d_ready = sem("d_ready")
        d_masked = sem("d_masked")
        s_ready = sem("s_ready")
        ktok_ready = sem("ktok_ready")
        num_done = sem("num_done")
        ss_ready = sem("ss_ready")
        ms_ready = sem("ms_ready")
        rms_ready = sem("rms_ready")
        f_ready = sem("f_ready")
        hs_ready = sem("hs_ready")
        state_done = sem("state_done")
        c_updated = sem("c_updated")
        gated = sem("gated")
        x_in = sem("x_in")
        tr_done = sem("tr_done")
        tr_evac = sem("tr_evac")
        ut_hi = sem("ut_hi")
        ut_ready = sem("ut_ready")
        moments_ready = sem("moments_ready")
        ln_ready = sem("ln_ready")
        xhat_ready = sem("xhat_ready")
        rows_in = sem("rows_in")
        h_written = sem("h_written")
        relu_sq = sem("relu_sq")
        h_hi = sem("h_hi")
        h_ready = sem("h_ready")
        rope_in = sem("rope_in")
        angle_ready = sem("angle_ready")
        sin_ready = sem("sin_ready")
        rope_ready = sem("rope_ready")
        att_in = sem("att_in")
        spilled = sem("spilled")
        roped = sem("roped")
        kt_done = sem("kt_done")
        kt_evac = sem("kt_evac")
        side_t = sem("side_t")
        q_taken = sem("q_taken")
        p_t = sem("p_t")
        p_taken = sem("p_taken")
        scores = sem("scores")
        max_ready = sem("max_ready")
        exp_ready = sem("exp_ready")
        pv_done = sem("pv_done")
        out_ready = sem("out_ready")
        at_hi = sem("at_hi")
        at_ready = sem("at_ready")
        resid_in = sem("resid_in")
        final_ready = sem("final_ready")
        stored = sem("stored")

        def fr(ap):
            return ap.bitcast(F32)

        class Steps:

            def __init__(self, eng, s):
                self.eng, self.sem, self.n = eng, s, 0

            def mark(self, ins):
                ins.then_inc(self.sem, 1)
                self.n += 1
                self.eng.wait_ge(self.sem, self.n)

        def wait_evac(eng, g, i=0, per=0):
            if g < RING:
                return
            before = g - RING
            count, s = (ACT_BEFORE, act_evac) if ENGINES[before] == "A" else (DVE_BEFORE, dve_evac)
            eng.wait_ge(s, count[before] + 1 + per * i)

        def o_group(nh, t):
            return FIRST["o0"] + t if nh == 0 else FIRST["o1a" if t < 2 else "o1b"] + t - (0 if t < 2 else 2)

        def half_group(name, t):
            return FIRST[name + "a"] + t if t < 4 else FIRST[name + "b"] + t - 4

        def kv_group(t):
            return FIRST["kva"] + t if t < 3 else FIRST["kvb"] + t - 3

        def gate_exp(nh, t):
            if nh == 0:
                return scratch[:, t % 2, :]
            return (dmat if t % 2 == 0 else smat)[:].rearrange("p h n -> p (h n)")

        SIDE = [("q", 0), ("q", 1)]
        for n in range(UNITS + 1):
            if n % 2 == 1 and (n + 3) // 2 < UNITS // 2:
                SIDE.append(("q", (n + 3) // 2))
            if n % 2 == 0 and n >= 4:
                SIDE.append(("o", (n - 4) // 2))
        SIDE.append(("o", UNITS // 2 - 1))

        def loaded(eng, n, i=0, per=0):
            eng.wait_ge(stage_loaded[n % 2], 16 * (n // 2 + 1) + 8 * per * i)

        block = ctx.enter_context(nc.Block())

        @block.sync
        def _(sp):
            for n in range(2):
                sp.dma_start(stage[:, n, :], stream[n]).then_inc(stage_loaded[n], 16)
            with sp.Fori(1, N_LOADS // 2) as i:
                for b in range(2):
                    sp.wait_ge(loads_used, 2 * i + (b - 1))
                    sp.dma_start(stage[:, b, :], stream[2 * i + b]).then_inc(stage_loaded[b], 16)
            for t in range(T):
                sp.wait_ge(final_ready, t + 1)
                sp.dma_start(out[t * P:(t + 1) * P, :], resid[:, t, 0:D]).then_inc(stored, 16)
            sp.wait_ge(stored, 16 * T)

        @block.gpsimd
        def _(pool):
            step = Steps(pool, pool_step)
            step.mark(pool.memset(neghalf[:], -0.5))
            for c in range(T):
                pool.wait_ge(d_ready, c + 1)
                pool.affine_select(out=dmat[:], in_=dmat[:], compare_op=ALU.is_ge, fill=0.0, base=0,
                                   pattern=[[0, H], [1, P]], channel_multiplier=-1).then_inc(d_masked, 1)
                pool.wait_ge(ms_ready, c + 1)
                pool.tensor_tensor(mean, mean, neghalf[:], ALU.pow).then_inc(rms_ready, 1)
            pool.wait_ge(num_done, H * T)
            pool.wait_ge(state_done, H * (T - 1))
            for t in range(T):
                pool.dma_start(resid[:, t, 0:D], x[t * P:(t + 1) * P, :]).then_inc(x_in, 16)

            def rows(j, scale):
                for r, src in enumerate(("ln_g", "ln_b")):
                    pool.dma_start(lnrows[:, r, :], consts[src][j].partition_broadcast(P)).then_inc(rows_in, 16)
                if scale:
                    pool.wait_ge(rows_in, 32 * (j + 1))
                    step.mark(pool.tensor_scalar(lnrows[:], lnrows[:], ALPHA, None, ALU.mult))

            def norm_scale(ln, t):
                j = t % 2
                pool.wait_ge(moments_ready, T * ln + t + 1)
                step.mark(pool.tensor_scalar(rstd[:, j, :], moments[:, j, 1:2], LN_EPS, None, ALU.add))
                step.mark(pool.tensor_tensor(rstd[:, j, :], rstd[:, j, :], neghalf[:, 0:1], ALU.pow))
                pool.tensor_scalar(nmr[:, j, :], moments[:, j, 0:1], -1.0, rstd[:, j, :], ALU.mult,
                                   ALU.mult).then_inc(ln_ready, 1)

            def write_h(t, event):
                pool.wait_ge(tr_done, 2 * (event + t) + 2)
                step.mark(pool.tensor_tensor(resid[:, t, 0:D], resid[:, t, 0:D], lnrows[:, 0, :], ALU.mult))
                pool.tensor_tensor(resid[:, t, 0:D], resid[:, t, 0:D], lnrows[:, 1, :],
                                   ALU.add).then_inc(h_written, 1)

            pool.wait_ge(hs_ready, T)
            pool.dma_start(sinks[:], consts["sinks"].partition_broadcast(P)).then_inc(rope_in, 16)
            pool.dma_start(posi[:], consts["positions"]).then_inc(rope_in, 16)
            pool.dma_start(turns[:, 0, :], consts["inv_freq"].partition_broadcast(P)).then_inc(rope_in, 16)
            pool.wait_ge(gated, 2 * T)
            rows(0, True)
            for t in range(T + LAG):
                if t < T:
                    norm_scale(0, t)
                if t >= LAG:
                    write_h(t - LAG, TR_LN0)
            pool.wait_ge(h_written, T)
            rows(1, True)
            for t in range(T + LAG):
                if t < T:
                    norm_scale(1, t)
                if t >= LAG:
                    write_h(t - LAG, TR_KV)
                    pool.wait_ge(h_written, T + t - LAG + 1)
                    pool.dma_start(resid_dram[t - LAG], resid[:, t - LAG, 0:D]).then_inc(spilled, 16)
            pool.wait_ge(group_done, FIRST["kva"])
            pool.dma_start(mask[:], consts["mask"]).then_inc(att_in, 16)
            for t in range(T):
                pool.wait_ge(side_t, SIDE.index(("o", 2 * t + 1)) + 1)
                pool.dma_start(resid[:, t, 0:D], resid_dram[t]).then_inc(resid_in, 16)
            pool.wait_ge(pv_done, UNITS)
            rows(2, True)
            for t in range(T + LAG):
                if t < T:
                    norm_scale(2, t)
                if t >= LAG:
                    write_h(t - LAG, TR_LN2)
            pool.wait_ge(h_written, 3 * T)
            rows(3, False)
            for t in range(T):
                norm_scale(3, t)

        @block.scalar
        def _(act):
            for dst, name in ((ident[:], "ident"), (mods[:], "mod_bias"), (fcols[:], "fcols"),
                              (cs[:, 0, :], "c"), (gw[:], "gate_w")):
                act.dma_start(dst, consts[name]).then_inc(consts_in, 16)
            act.dma_start(gt[:, 0, :], consts["gate_b"].partition_broadcast(P)).then_inc(consts_in, 16)
            for k in range(K):
                act.dma_start(resid[:, k, 0:S], xt[k]).then_inc(xt_in, 16)
            act.wait_ge(consts_in, 96)
            act.activation(cs[:, 1, :], cs[:, 0, :], ACT.Exp, scale=-1.0).then_inc(gate_e, 1)
            act.activation(gwhi[:], gw[:], ACT.Copy).then_inc(gate_e, 1)

            def split(n, w, i=0, per=0):
                if is_scaled(w):
                    act.wait_ge(scaled, SCALED_BEFORE[n] + 1 + 4 * i)
                else:
                    loaded(act, n, i, per)
                former = former_in_slot(w)
                if former is not None:
                    act.wait_ge(group_done, groups_through(former) + 24 * i)
                act.activation(whi[:, slot_of(w), :], stage[:, n % 2, :], ACT.Copy).then_inc(hi_ready, 1)

            def splits(*blocks):
                for w in blocks:
                    split(NUMBER["w", w], w)

            def first_u(half):
                cut = slice(half * HALF, (half + 1) * HALF)
                for k in range(K):
                    act.wait_ge(u_made, K * half + k + 1)
                    act.activation(uhi[:, k, cut], resid[:, k, cut], ACT.Copy).then_inc(u_hi, 1)

            splits(0)
            first_u(0)
            splits(1)
            first_u(1)
            splits(2, 3, 4, 5)

            def evac_qk(n):
                for half in range(2):
                    g = FIRST["qk"] + 2 * n + half
                    act.wait_ge(group_done, g + 1)
                    act.activation(qk[:, 4 * half:4 * half + 4, n * P:(n + 1) * P],
                                   ps[:, g % RING, :].rearrange("p (c t) -> p c t", c=4), ACT.Copy,
                                   scale=1.0 if n < H else 1.0 / math.sqrt(P)).then_inc(act_evac, 1)

            evac_qk(0)
            act.wait_ge(gate_v, 3)
            act.activation(gt[:, 2, :], gt[:, 1, :], ACT.Tanh, scale=1.0 / CAP).then_inc(gate_e, 1)
            act.wait_ge(gate_v, 4)
            act.activation(gt[:, 2, 0:HC], gt[:, 1, HC:2 * HC], ACT.Exp, scale=-1.0).then_inc(gate_e, 1)
            act.wait_ge(gate_v, 5)
            act.activation(gt[:, 3, 0:HC], gt[:, 2, HC:2 * HC], ACT.Ln).then_inc(gate_e, 1)
            splits(6)
            evac_qk(1)
            splits(7)
            evac_qk(2)
            splits(8)
            evac_qk(3)
            splits(9)
            row = scratch[0:HC].rearrange("p a (b n) -> p (a b) n", n=P)
            act.wait_ge(gate_v, 10)
            act.activation(winter[:], row[:, 4, :], ACT.Exp, scale=-1.0, bias=m_prev_col)
            act.activation(row[:, 5, :], row[:, 3, :], ACT.Exp, bias=negm[:, P - 1:P])
            act.activation(row[:, 6, :], row[:, 7, :], ACT.Exp, scale=-1.0).then_inc(gate_e, 1)
            evac_qk(4)
            splits(10)
            for n, w in ((5, 11), (6, 12), (7, 13)):
                evac_qk(n)
                splits(w)
            splits(14, 15, 16, 18, 17, 19, 20, 21)

            def evac_o(nh, t):
                act.wait_ge(group_done, o_group(nh, t) + 1)
                if t >= 2:
                    act.wait_ge(gated, T * nh + t - 1)
                act.activation(gate_exp(nh, t), ps[:, o_group(nh, t) % RING, :], ACT.Exp,
                               scale=-1.0).then_inc(act_evac, 1)

            for c in range(T):
                act.wait_ge(mix, 4 * c + 1)
                for h in range(H):
                    last = act.activation(dmat[:, h, :], ps[:, X, h * P:(h + 1) * P], ACT.Exp,
                                          bias=cols[:, 0, h * T + c:h * T + c + 1])
                last.then_inc(d_ready, 1)
                act.wait_ge(mix, 4 * c + 4)
                for h in range(H):
                    last = act.activation(ktok[:, h, :], ps[:, X + 2, h * P:(h + 1) * P], ACT.Copy,
                                          scale=cols[:, 2, h * T + c:h * T + c + 1])
                last.then_inc(ktok_ready, 1)
                act.wait_ge(s_ready, 2 * c + 2)
                for h in range(H):
                    act.wait_ge(num_done, H * c + h + 1)
                    if h >= 2:
                        act.wait_ge(ss_ready, H * c + h - 1)
                    act.activation(dmat[:, h % 2 * 2:h % 2 * 2 + 2, :],
                                   ps[:, X + h, 0:DV].rearrange("p (a b) -> p a b", a=2), ACT.Square,
                                   accum_out=sumsq[:, h:h + 1]).then_inc(ss_ready, 1)
                act.wait_ge(f_ready, c + 1)
                for h in range(H):
                    last = act.activation(qk[:, c, h * DV:(h + 1) * DV], ps[:, X + h, 0:DV], ACT.Copy,
                                          scale=factor[:, h:h + 1])
                last.then_inc(hs_ready, 1)
                if c:
                    evac_o(0, c - 1)
            evac_o(0, T - 1)
            splits(22, 23)

            def make_u(event, t, mul, add):
                for j in range(2):
                    n = 2 * (event + t) + j
                    act.wait_ge(tr_done, n + 1)
                    if n >= 2:
                        act.wait_ge(ut_ready, n - 1)
                    for k in range(4):
                        kk = 4 * j + k
                        last = act.activation(scratch[:, j, k * P:(k + 1) * P],
                                              ps[:, X + n % 4, k * P:(k + 1) * P], ACT.Identity,
                                              scale=mul[:, kk:kk + 1],
                                              bias=0.0 if add is None else add[:, kk:kk + 1])
                    last.then_inc(tr_evac, 1)
                    act.wait_ge(tr_evac, n + 1)
                    act.activation(uhi[:, 4 * j:4 * j + 4, t * P:(t + 1) * P],
                                   scratch[:, j, :].rearrange("p (k n) -> p k n", k=4),
                                   ACT.Copy).then_inc(ut_hi, 1)

            def make_gate_row(g):
                for half in range(2):
                    act.wait_ge(group_done, g + half + 1)
                    act.activation(gate_row[:, half * HALF:(half + 1) * HALF], ps[:, (g + half) % RING, :],
                                   ACT.Identity, bias=ones[:, 0:1]).then_inc(act_evac, 1)

            def make_xhat(ln, t):
                act.wait_ge(ln_ready, T * ln + t + 1)
                act.activation(resid[:, t, 0:D], resid[:, t, 0:D], ACT.Identity,
                               scale=rstd[:, t % 2, :], bias=nmr[:, t % 2, :]).then_inc(xhat_ready, 1)

            act.wait_ge(gated, T)
            for t in range(T):
                if t == T - 1:
                    splits(26, 27, 28, 29)
                evac_o(1, t)
                if t == 1:
                    make_gate_row(FIRST["gm0"])
                if t == 4:
                    splits(24, 25)
                if t >= 1:
                    make_u(TR_HS, t - 1, fcols[:, 6, :], None)
            make_u(TR_HS, T - 1, fcols[:, 6, :], None)
            splits(30, 31)

            for t in range(T):
                make_xhat(0, t)
                if t == 4:
                    make_gate_row(FIRST["gf0"])
                    splits(32, 33)
                if t >= LAG:
                    make_u(TR_LN0, t - LAG, mulv[:, 1, :], addv[:, 1, :])
            for t in range(T - LAG, T):
                make_u(TR_LN0, t, mulv[:, 1, :], addv[:, 1, :])

            def mlp_up(first, w0, load0, h0, i=0, per=0):
                for u in range(8):
                    f, half = u // 2, u % 2
                    act.wait_ge(group_done, first + u + 1 + 24 * i)
                    if u >= 2:
                        act.wait_ge(h_ready, h0 + u - 1 + 8 * i)
                    act.activation(scratch[:, u % 2, :], ps[:, (first + u) % RING, :],
                                   ACT.Relu).then_inc(act_evac, 1)
                    act.wait_ge(relu_sq, h0 + u + 1 + 8 * i)
                    act.activation(hhi[:, f, half * HALF:(half + 1) * HALF], scratch[:, u % 2, :],
                                   ACT.Copy).then_inc(h_hi, 1)
                    if w0 + CHUNK_LOADS[u] < N_W:
                        split(load0 + u, w0 + CHUNK_LOADS[u], i, per)

            end = CHUNKS - 1
            act.wait_ge(ut_ready, 2 * (TR_LN0 + T))
            with act.Fori(0, end) as i:
                mlp_up(FIRST["mlp0"], W_MLP0, LOADS_MLP0, 0, i, 16)
            act.wait_ge(angle_ready, 1)
            act.activation(rope[:, :, ROT + RH:2 * ROT], angle[:], ACT.Sin)
            act.activation(rope[:, :, 0:RH], turns[:], ACT.Sin).then_inc(sin_ready, 1)
            mlp_up(FIRST["mlp0"] + 24 * end, W_MLP0 + 8 * end, LOADS_MLP0 + 16 * end, 8 * end)
            act.wait_ge(h_ready, 8 * CHUNKS)
            for t in range(T):
                make_xhat(1, t)
                if t >= LAG:
                    make_u(TR_KV, t - LAG, mulv[:, 2, :], addv[:, 2, :])
            splits(98, 99)
            for t in range(T - LAG, T):
                make_u(TR_KV, t, mulv[:, 2, :], addv[:, 2, :])
            splits(100, 101)

            def evac_kt(t):
                act.wait_ge(kt_done, t + 1)
                act.activation(kt[:, :, t * P:(t + 1) * P],
                               ps[:, M, 0:2 * P].rearrange("p (m n) -> p m n", m=2), ACT.Copy).then_inc(kt_evac, 1)

            for t in range(T):
                if t == 3:
                    make_gate_row(FIRST["gm1"])
                if t >= 1:
                    evac_kt(t - 1)
                    make_u(TR_Q, t - 1, mulv[:, 3, :], addv[:, 3, :])
            splits(102, 103)
            evac_kt(T - 1)
            make_u(TR_Q, T - 1, mulv[:, 3, :], addv[:, 3, :])
            splits(104, 105, 106, 107, 108, 109)

            def take_q(pair):
                m = pair % 2
                act.wait_ge(side_t, SIDE.index(("q", pair)) + 1)
                if pair >= 2:
                    act.wait_ge(scores, 2 * pair - 2)
                act.activation(acc[:, m * HALF:(m + 1) * HALF], ps[:, X + 3, :], ACT.Copy,
                               scale=1.0 / math.sqrt(HD)).then_inc(q_taken, 1)

            def exps(n):
                lo, small = P if n < 4 else 0, att[:, n % 3]
                act.wait_ge(max_ready, n + 1)
                for g in range(GROUP):
                    act.activation(probs[:, n % 3, g, lo:], probs[:, n % 3, g, lo:], ACT.Exp,
                                   bias=small[:, 1, g:g + 1], accum_out=small[:, 2, g:g + 1])
                act.activation(small[:, 4, :], small[:, 3, :], ACT.Exp).then_inc(exp_ready, 1)

            def take_pt(n):
                act.wait_ge(p_t, n + 1)
                if n >= 2:
                    act.wait_ge(pv_done, n - 1)
                for j in range(1 if n < 4 else 0, 2):
                    last = act.activation(probst[:, n % 2, j, :], ps[:, X + j, :], ACT.Copy)
                last.then_inc(p_taken, 1)

            def out_hi(pair):
                b, m = pair // 2, pair % 2
                act.wait_ge(side_t, SIDE.index(("o", pair)) + 1)
                act.activation(uhi[:, 4 * m:4 * m + 4, b * P:(b + 1) * P],
                               ps[:, X + 3, :].rearrange("p (k n) -> p k n", k=4), ACT.Copy).then_inc(at_hi, 1)

            def side(n):
                if n % 2 == 1 and (n + 3) // 2 < UNITS // 2:
                    take_q((n + 3) // 2)
                if n % 2 == 0 and n >= 4:
                    out_hi((n - 4) // 2)

            take_q(0)
            take_q(1)
            exps(0)
            for n in range(UNITS):
                if n + 1 < UNITS:
                    exps(n + 1)
                take_pt(n)
                if n < 4:
                    splits((110, 111, 114, 115)[n])
                side(n)
            side(UNITS)
            out_hi(UNITS // 2 - 1)
            splits(112, 113)

            for t in range(T):
                make_xhat(2, t)
                if t == 4:
                    make_gate_row(FIRST["gf1"])
                    splits(116, 117)
                if t >= LAG:
                    make_u(TR_LN2, t - LAG, mulv[:, 4, :], addv[:, 4, :])
            for t in range(T - LAG, T):
                make_u(TR_LN2, t, mulv[:, 4, :], addv[:, 4, :])
            act.wait_ge(ut_ready, 2 * (TR_LN2 + T))
            with act.Fori(0, end) as i:
                mlp_up(FIRST["mlp1"], W_MLP1, LOADS_MLP1, 8 * CHUNKS, i, 8)
            mlp_up(FIRST["mlp1"] + 24 * end, W_MLP1 + 8 * end, LOADS_MLP1 + 8 * end, 8 * CHUNKS + 8 * end)
            for t in range(T):
                make_xhat(3, t)

        @block.vector
        def _(v):
            step = Steps(v, dve_step)
            v.memset(ones[:], 1.0).then_inc(gate_v, 1)
            v.wait_ge(gate_e, 1)
            step.mark(v.tensor_scalar(cs[:, 1, :], cs[:, 1, :], 1.0, None, ALU.add))
            step.mark(v.reciprocal(cs[:, 1, :], cs[:, 1, :]))
            step.mark(v.tensor_tensor(cs[:, 0, :], cs[:, 0, :], cs[:, 1, :], ALU.mult))
            v.wait_ge(gate_e, 2)
            v.tensor_tensor(gwlo[:], gw[:], fr(gwhi[:]), ALU.subtract).then_inc(gate_v, 1)

            def ada(n, k, i=0, per=0):
                loaded(v, n, i, per)
                if k == 0:
                    ins = v.tensor_scalar(acc[:], stage[:, n % 2, :], cs[:, 0, 0:1], None, ALU.mult)
                else:
                    v.wait_ge(loads_used, n + per * i)
                    ins = v.scalar_tensor_tensor(acc[:], stage[:, n % 2, :], cs[:, 0, k:k + 1], acc[:],
                                                 ALU.mult, ALU.add)
                ins.then_inc(loads_used, 1)

            def adas(vec, ks=range(K)):
                for k in ks:
                    if k == 0 and vec:
                        v.wait_ge(sum_done, vec)
                    ada(NUMBER["ada", vec, k], k)

            def take_mod(vec, i=0):
                v.wait_ge(sum_done, vec + 1 + i)
                dst = mods[:, vec + i, :]
                v.tensor_tensor(dst, ps[:, M, 0:K], dst, ALU.add).then_inc(sum_read, 1)

            def scale(n, w, i=0, per=0):
                if is_scaled(w):
                    loaded(v, n, i, per)
                    src = stage[:, n % 2, :]
                    gate = gate_row[:, 0:D]
                    if W_OUT <= w < W_MLP0 or W_OP <= w < W_MLP1:
                        nh = (w - W_OUT if w < W_MLP0 else w - W_OP) // 4
                        src = src.rearrange("p (k n) -> p k n", k=2)
                        gate = gate[:, nh * HALF:(nh + 1) * HALF].unsqueeze(1).to_broadcast([P, 2, HALF])
                    v.tensor_tensor(src, src, gate, ALU.mult).then_inc(scaled, 1)

            def low(n, w, i=0, per=0):
                v.wait_ge(hi_ready, WEIGHTS_BEFORE[n] + 1 + 8 * i)
                v.tensor_tensor(wlo[:, slot_of(w), :], stage[:, n % 2, :], fr(whi[:, slot_of(w), :]),
                                ALU.subtract).then_inc(loads_used, 1)

            def preps(*blocks):
                for w in blocks:
                    scale(NUMBER["w", w], w)
                    low(NUMBER["w", w], w)

            def modulation(j, sc, sh, ln=None, inv=1.0):
                v.wait_ge(sum_read, max(sc, sh) + 1)
                step.mark(v.tensor_scalar(mulv[:, j, :], mods[:, sc, :], 1.0, inv, ALU.add, ALU.mult))
                if ln is None:
                    step.mark(v.tensor_copy(addv[:, j, :], mods[:, sh, :]))
                    return
                step.mark(v.tensor_tensor(addv[:, j, :], mulv[:, j, :], fcols[:, 3 + ln, :], ALU.mult))
                step.mark(v.tensor_tensor(addv[:, j, :], addv[:, j, :], mods[:, sh, :], ALU.add))
                step.mark(v.tensor_tensor(mulv[:, j, :], mulv[:, j, :], fcols[:, ln, :], ALU.mult))

            def first_u(half):
                cut = slice(half * HALF, (half + 1) * HALF)
                for k in range(K):
                    v.tensor_scalar(resid[:, k, cut], resid[:, k, cut], mulv[:, 0, k:k + 1], addv[:, 0, k:k + 1],
                                    ALU.mult, ALU.add).then_inc(u_made, 1)
                for k in range(K):
                    v.wait_ge(u_hi, K * half + k + 1)
                    v.tensor_tensor(ulo[:, k, cut], resid[:, k, cut], fr(uhi[:, k, cut]),
                                    ALU.subtract).then_inc(u_ready, 1)

            adas(SC_M0)
            take_mod(SC_M0)
            adas(SH_M0)
            take_mod(SH_M0)
            modulation(0, SC_M0, SH_M0)
            v.wait_ge(xt_in, 16 * K)
            preps(0)
            first_u(0)
            preps(1)
            first_u(1)
            preps(2, 3, 4, 5)

            v.wait_ge(gate_m, 1)
            v.tensor_tensor(gt[:, 1, :].rearrange("p (g t) -> p g t", t=T),
                            ps[:, M, 0:T * 8].rearrange("p (t g) -> p g t", g=8),
                            gt[:, 0, :].rearrange("p (g t) -> p g t", t=T), ALU.add).then_inc(gate_v, 1)
            v.wait_ge(gate_e, 3)
            v.tensor_scalar(gt[:, 1, :], gt[:, 2, :], CAP, None, ALU.mult).then_inc(gate_v, 1)
            v.wait_ge(gate_e, 4)
            e, e1, rest, log = gt[:, 2, 0:HC], gt[:, 2, HC:2 * HC], gt[:, 3, HC:2 * HC], gt[:, 3, 0:HC]
            v.tensor_scalar(e1, e, 1.0, None, ALU.add).then_inc(gate_v, 1)
            v.wait_ge(gate_v, 5)
            step.mark(v.tensor_scalar(rest, e1, -1.0, None, ALU.add))
            step.mark(v.tensor_tensor(rest, e, rest, ALU.subtract))
            v.wait_ge(gate_e, 5)
            step.mark(v.reciprocal(e1, e1))
            step.mark(v.tensor_tensor(rest, rest, e1, ALU.mult))
            step.mark(v.tensor_tensor(log, log, rest, ALU.add))
            v.tensor_scalar(gt[:, 1, HC:2 * HC], log, -1.0, None, ALU.mult).then_inc(gate_v, 1)
            preps(6)
            row = scratch[0:HC].rearrange("p a (b n) -> p (a b) n", n=P)
            v.memset(row[:, 7, :], 0.0)
            v.wait_ge(gate_m, 2)
            step.mark(v.tensor_copy(row[:, 0:2, :], ps[0:HC, M, 0:2 * P].rearrange("p (a n) -> p a n", a=2)))
            step.mark(v.tensor_tensor_scan(row[:, 2, :], row[:, 1, :], row[:, 7, :], 0.0, ALU.add, ALU.add))
            step.mark(v.tensor_tensor(row[:, 3, :], row[:, 0, :], row[:, 2, :], ALU.subtract))
            v.tensor_tensor_scan(row[:, 4, :], row[:, 3, :], row[:, 3, :], MASKED, ALU.max,
                                 ALU.max).then_inc(gate_v, 1)
            preps(7)
            ends, sums = gt[0:1, 3, 0:HC], gt[0:1, 3, HC:2 * HC]
            m_row, m_prev = gt[0:1, 2, 0:HC], gt[0:1, 2, HC:2 * HC]
            v.wait_ge(gate_m, 3)
            step.mark(v.tensor_copy(gt[0:1, 3, :], ps[0:1, M, 0:2 * HC]))
            step.mark(v.tensor_tensor(sums, ends, sums, ALU.add))
            for h in range(H):
                part = slice(h * T, (h + 1) * T)
                step.mark(v.tensor_tensor_scan(m_row[:, part], ends[:, part], sums[:, part], 0.0,
                                               ALU.add, ALU.max))
            step.mark(v.memset(m_prev, 0.0))
            v.tensor_copy(m_prev.rearrange("p (h t) -> p h t", t=T)[:, :, 1:T],
                          m_row.rearrange("p (h t) -> p h t", t=T)[:, :, 0:T - 1]).then_inc(gate_v, 1)
            preps(8)
            v.wait_ge(gate_m, 4)
            step.mark(v.tensor_copy(m_prev_col, ps[0:HC, M, 0:1]))
            step.mark(v.tensor_scalar(row[:, 4, :], row[:, 4, :], m_prev_col, None, ALU.max))
            v.tensor_scalar(negm[:], row[:, 4, :], -1.0, None, ALU.mult).then_inc(gate_v, 1)
            v.tensor_tensor(row[:, 7, :], row[:, 2, :], row[:, 4, :], ALU.add).then_inc(gate_v, 1)
            preps(9)
            v.memset(cstate[:], 0.0)
            v.wait_ge(gate_m, 5)
            v.tensor_copy(cols[:], ps[:, M, 0:5 * HC].rearrange("p (a n) -> p a n", a=5)).then_inc(gate_v, 1)
            preps(10)
            adas(G_M0)
            v.memset(resid[:].rearrange("p t (h n) -> p t h n", h=H)[:, :, :, DV:DV + 1], 1.0)
            preps(11, 12, 13)
            take_mod(G_M0)

            def evac_v(nh, t):
                g = FIRST["v"] + T * nh + t
                v.wait_ge(group_done, g + 1)
                dst = resid[:, t, :].rearrange("p (h n) -> p h n", h=H)[:, 2 * nh:2 * nh + 2, 0:DV]
                v.tensor_copy(dst, ps[:, g % RING, :].rearrange("p (h n) -> p h n", h=2)).then_inc(dve_evac, 1)

            def ada_pair(vecs, t):
                adas(vecs[t // 4], range(2 * (t % 4), 2 * (t % 4) + 2))

            for t in range(T):
                if t == T - 1:
                    preps(14, 15)
                evac_v(0, t)
                ada_pair((SH_F0, SC_F0), t)
                if t == 5:
                    take_mod(SH_F0)
            for t in range(T):
                if t == T - 1:
                    preps(18, 17, 19)
                evac_v(1, t)
                ada_pair((G_F0, SH_KV), t)
                if t == 1:
                    preps(16)
                    take_mod(SC_F0)
                if t == 5:
                    take_mod(G_F0)
            preps(20, 21)

            def apply_gate(nh, t):
                e = gate_exp(nh, t)
                v.wait_ge(act_evac, ACT_BEFORE[o_group(nh, t)] + 1)
                step.mark(v.tensor_scalar(e, e, 1.0, None, ALU.add))
                step.mark(v.reciprocal(e, e))
                v.wait_ge(hs_ready, t + 1)
                part = qk[:, t, nh * HALF:(nh + 1) * HALF]
                v.tensor_tensor(part, part, e, ALU.mult).then_inc(gated, 1)

            for c in range(T):
                v.wait_ge(mix, 4 * c + 3)
                v.tensor_tensor(qk[:, c, 0:H * P], ps[:, X + 3, :], qk[:, c, 0:H * P], ALU.mult).then_inc(s_ready, 1)
                v.wait_ge(d_masked, c + 1)
                v.tensor_tensor(smat[:].rearrange("p h n -> p (h n)"), ps[:, X + 1, :],
                                dmat[:].rearrange("p h n -> p (h n)"), ALU.mult).then_inc(s_ready, 1)
                r = stats[:, 0, 0:H]
                v.wait_ge(ss_ready, H * (c + 1))
                step.mark(v.tensor_copy(r, ps[:, X:X + H, DV]))
                step.mark(v.scalar_tensor_tensor(r, r, -1.0, r, ALU.mult, ALU.max))
                step.mark(v.tensor_tensor(r, r, cols[:, 3, :].rearrange("p (h t) -> p h t", t=T)[:, :, c],
                                          ALU.max))
                step.mark(v.reciprocal(r, r))
                step.mark(v.tensor_tensor(mean, sumsq, r, ALU.mult))
                step.mark(v.tensor_tensor(mean, mean, r, ALU.mult))
                v.tensor_scalar(mean, mean, 1.0 / DV, RMS_EPS, ALU.mult, ALU.add).then_inc(ms_ready, 1)
                v.wait_ge(rms_ready, c + 1)
                v.tensor_tensor(factor, mean, r, ALU.mult).then_inc(f_ready, 1)
                if c:
                    apply_gate(0, c - 1)
                if c < T - 1:
                    for h in range(H):
                        v.wait_ge(state_done, H * c + h + 1)
                        v.scalar_tensor_tensor(cstate[:, h, :], cstate[:, h, :],
                                               cols[:, 4, h * T + c:h * T + c + 1],
                                               ps[:, X + h, 0:DV + 1], ALU.mult, ALU.add).then_inc(c_updated, 1)
            take_mod(SH_KV)
            apply_gate(0, T - 1)
            preps(22, 23)

            def diagonal(vec):
                v.wait_ge(sum_read, vec + 1)
                for k in range(K):
                    last = v.tensor_scalar(acc[:, k * P:(k + 1) * P], ident[:], mods[:, vec, k:k + 1], None,
                                           ALU.mult)
                last.then_inc(diag_ready, 1)

            def gate_row_made(name):
                v.wait_ge(act_evac, ACT_BEFORE[FIRST[name] + 2])

            def make_lo(event, t):
                for j in range(2):
                    v.wait_ge(ut_hi, 2 * (event + t) + j + 1)
                    cut = slice(t * P, (t + 1) * P)
                    v.tensor_tensor(ulo[:, 4 * j:4 * j + 4, cut],
                                    scratch[:, j, :].rearrange("p (k n) -> p k n", k=4),
                                    fr(uhi[:, 4 * j:4 * j + 4, cut]), ALU.subtract).then_inc(ut_ready, 1)

            diagonal(G_M0)
            for t in range(T):
                if t == 4:
                    gate_row_made("gm0")
                    preps(24, 25)
                if t == T - 1:
                    preps(26, 27, 28, 29)
                apply_gate(1, t)
                if t >= 1:
                    make_lo(TR_HS, t - 1)
            make_lo(TR_HS, T - 1)

            def norm(ln, t):
                j = t % 2
                if t >= LAG:
                    v.wait_ge(xhat_ready, T * ln + t - 1)
                for half in range(2):
                    step.mark(v.bn_stats(stats[:, j, 6 * half:6 * half + 6],
                                         resid[:, t, half * HALF:(half + 1) * HALF]))
                v.bn_aggr(moments[:, j, :], stats[:, j, :]).then_inc(moments_ready, 1)

            def add_out(g, t, nh, alpha):
                v.wait_ge(group_done, g + 1)
                dst = resid[:, t, nh * HALF:(nh + 1) * HALF]
                v.scalar_tensor_tensor(dst, dst, alpha, ps[:, g % RING, :], ALU.mult,
                                       ALU.add).then_inc(dve_evac, 1)

            v.wait_ge(x_in, 16 * T)
            for t in range(T):
                if t == T - 1:
                    preps(30, 31)
                add_out(FIRST["out0"] + t, t, 0, ALPHA)
            modulation(1, SC_F0, SH_F0, ln=0)
            diagonal(G_F0)
            for t in range(T):
                g = half_group("out1", t)
                add_out(g, t, 1, ALPHA)
                v.wait_ge(dve_evac, DVE_BEFORE[g] + 1)
                norm(0, t)
                if t == 4:
                    gate_row_made("gf0")
                    preps(32, 33)
                if t >= LAG:
                    make_lo(TR_LN0, t - LAG)
            for t in range(T - LAG, T):
                make_lo(TR_LN0, t)

            def angles():
                v.wait_ge(rope_in, 48)
                pos = rope[:, 0, 0:T]
                step.mark(v.tensor_copy(pos, posi[:]))
                step.mark(v.tensor_tensor(angle[:], pos.unsqueeze(2).to_broadcast([P, T, RH]),
                                          turns[:, 0, :].unsqueeze(1).to_broadcast([P, T, RH]), ALU.mult))
                step.mark(v.tensor_scalar(turns[:], angle[:], 1.0 / (2 * math.pi), ROUNDER, ALU.mult, ALU.add))
                step.mark(v.tensor_scalar(turns[:], turns[:], -ROUNDER, None, ALU.add))
                for part in TWO_PI:
                    step.mark(v.scalar_tensor_tensor(angle[:], turns[:], -part, angle[:], ALU.mult, ALU.add))
                step.mark(v.tensor_scalar(angle[:], angle[:], PI_IN, -PI_IN, ALU.min, ALU.max))
                step.mark(v.tensor_scalar(turns[:], angle[:], math.pi / 2, None, ALU.add))
                wrap = rope[:, :, 0:RH]
                step.mark(v.tensor_scalar(wrap, turns[:], math.pi, -2 * math.pi, ALU.is_gt, ALU.mult))
                step.mark(v.tensor_tensor(turns[:], turns[:], wrap, ALU.add))
                v.tensor_scalar(turns[:], turns[:], PI_IN, -PI_IN, ALU.min, ALU.max).then_inc(angle_ready, 1)

            def mlp_chunk(first, w0, load0, h0, i=0, per=0, with_ada=False, tail=None):
                for u in range(8):
                    f, half = u // 2, u % 2
                    q = scratch[:, u % 2, :]
                    w = w0 + CHUNK_LOADS[u]
                    v.wait_ge(act_evac, ACT_BEFORE[first + u] + 1 + 8 * i)
                    v.tensor_tensor(q, q, q, ALU.mult).then_inc(relu_sq, 1)
                    if w < N_W:
                        scale(load0 + u, w, i, per)
                    v.wait_ge(h_hi, h0 + u + 1 + 8 * i)
                    cut = slice(half * HALF, (half + 1) * HALF)
                    v.tensor_tensor(hlo[:, f, cut], q, fr(hhi[:, f, cut]), ALU.subtract).then_inc(h_ready, 1)
                    if w < N_W:
                        low(load0 + u, w, i, per)
                for d in range(16):
                    t, nh = d // 2, d % 2
                    g = first + 8 + d
                    v.wait_ge(group_done, g + 1 + 24 * i)
                    v.wait_ge(dve_evac, DVE_BEFORE[g] - 15 + 16 * i)
                    dst = resid[:, t, nh * HALF:(nh + 1) * HALF]
                    v.tensor_tensor(dst, ps[:, g % RING, :], dst, ALU.add).then_inc(dve_evac, 1)
                    if with_ada and 1 <= d <= K:
                        if d == 1:
                            v.wait_ge(sum_done, SC_KV + i)
                        ada(load0 + 8 + d - 1, d - 1, i, per)
                    if with_ada and d == 14:
                        take_mod(SC_KV, i)
                    if tail and nh == 1:
                        v.wait_ge(dve_evac, DVE_BEFORE[g] + 1)
                        tail(t)

            v.wait_ge(h_written, T)
            end = CHUNKS - 1
            with v.Fori(0, end) as i:
                mlp_chunk(FIRST["mlp0"], W_MLP0, LOADS_MLP0, 0, i, 16, with_ada=True)
            angles()
            modulation(2, SC_KV, SH_KV, ln=1)
            modulation(3, SC_M1, SH_M1, inv=1.0 / ALPHA)
            modulation(4, SC_F1, SH_F1, ln=2)

            def tail_kv(t):
                norm(1, t)
                if t >= LAG:
                    make_lo(TR_KV, t - LAG)

            mlp_chunk(FIRST["mlp0"] + 24 * end, W_MLP0 + 8 * end, LOADS_MLP0 + 16 * end, 8 * end, tail=tail_kv)
            preps(98, 99)
            for t in range(T - LAG, T):
                make_lo(TR_KV, t)
            preps(100, 101)

            v.wait_ge(sin_ready, 1)
            v.tensor_copy(rope[:, :, RH:ROT], rope[:, :, 0:RH])
            step.mark(v.tensor_scalar(rope[:, :, ROT:ROT + RH], rope[:, :, ROT + RH:2 * ROT], -1.0, None, ALU.mult))

            def rotate(src, dst, heads, t):
                def table(a, n):
                    return rope[:, t, a:a + n].unsqueeze(1).to_broadcast([P, heads, n])

                part = rtmp[:, :, 0:heads, :]
                step.mark(v.tensor_copy(dst, src))
                v.tensor_tensor(part[:, 1, :, 0:RH], src[:, :, RH:ROT], table(ROT, RH), ALU.mult)
                step.mark(v.tensor_tensor(part[:, 1, :, RH:ROT], src[:, :, 0:RH], table(ROT + RH, RH), ALU.mult))
                ins = v.tensor_tensor(part[:, 0], src[:, :, 0:ROT], table(0, ROT), ALU.mult)
                ins.then_inc(dve_evac, 1)

            def finish_rotation(dst, heads):
                part = rtmp[:, :, 0:heads, :]
                v.tensor_tensor(dst[:, :, 0:ROT], part[:, 0], part[:, 1], ALU.add).then_inc(roped, 1)

            for t in range(T):
                g = kv_group(t)
                if t == 1:
                    diagonal(G_M1)
                if t == T - 1:
                    preps(102, 103)
                v.wait_ge(group_done, g + 1)
                src = ps[:, g % RING, :].rearrange("p (h d) -> p h d", d=HD)
                if t >= 2:
                    v.wait_ge(kt_done, t - 1)
                dst = probs[:, t % 2, 0, :].rearrange("p (h d) -> p h d", d=HD)
                step.mark(v.tensor_copy(vv[:, t, :], ps[:, g % RING, 4 * HD:8 * HD]))
                rotate(src[:, 0:4], dst, 4, t)
                v.wait_ge(dve_evac, DVE_BEFORE[g] + 1)
                finish_rotation(dst, 4)
                if t >= 1:
                    make_lo(TR_Q, t - 1)
            make_lo(TR_Q, T - 1)
            gate_row_made("gm1")
            preps(104, 105)
            v.wait_ge(spilled, 16 * T)
            for nh in range(2):
                for t in range(T):
                    g = FIRST["q"] + T * nh + t
                    if t == T - 1 and nh == 0:
                        preps(106, 107)
                    v.wait_ge(group_done, g + 1)
                    v.wait_ge(roped, T + T * nh + t)
                    dst = resid[:, t, nh * HALF:(nh + 1) * HALF].rearrange("p (h d) -> p h d", d=HD)
                    rotate(ps[:, g % RING, :].rearrange("p (h d) -> p h d", d=HD), dst, 8, t)
                    v.wait_ge(dve_evac, DVE_BEFORE[g] + 1)
                    finish_rotation(dst, 8)
                if nh == 0:
                    preps(108, 109)

            def maxima(n):
                lo, u = (P if n < 4 else 0), n % 4
                small = att[:, n % 3]
                v.wait_ge(scores, n + 1)
                if n >= 3:
                    v.wait_ge(p_t, n - 2)
                for g in range(GROUP):
                    bank, at = 2 * (n % 2) + g // 2, g % 2 * 2 * P
                    last = v.tensor_tensor_reduce(probs[:, n % 3, g, lo:], ps[:, bank, at + lo:at + 2 * P],
                                                  mask[:, lo:], 1.0, sinks[:, 4 * u + g:4 * u + g + 1],
                                                  ALU.add, ALU.max, small[:, 0, g:g + 1])
                step.mark(last)
                step.mark(v.tensor_scalar(small[:, 1, :], small[:, 0, :], -1.0, None, ALU.mult))
                v.tensor_tensor(small[:, 3, :], small[:, 1, :], sinks[:, 4 * u:4 * u + 4],
                                ALU.add).then_inc(max_ready, 1)

            def totals(n):
                small = att[:, n % 3]
                v.wait_ge(exp_ready, n + 1)
                step.mark(v.tensor_tensor(small[:, 5, :], small[:, 2, :], small[:, 4, :], ALU.add))
                step.mark(v.reciprocal(small[:, 5, :], small[:, 5, :]))

            def take_out(n):
                b, u = n // 4, n % 4
                v.wait_ge(pv_done, n + 1)
                dst = resid[:, b, u * GROUP * HD:(u + 1) * GROUP * HD].rearrange("p (g d) -> p g d", g=GROUP)
                v.tensor_tensor(dst, ps[:, X + 2, 0:GROUP * HD].rearrange("p (g d) -> p g d", g=GROUP),
                                att[:, n % 3, 5, :].unsqueeze(2).to_broadcast([P, GROUP, HD]),
                                ALU.mult).then_inc(out_ready, 1)

            def out_lo(pair):
                b, m = pair // 2, pair % 2
                cut = slice(b * P, (b + 1) * P)
                v.wait_ge(at_hi, pair + 1)
                v.tensor_tensor(ulo[:, 4 * m:4 * m + 4, cut], ps[:, X + 3, :].rearrange("p (k n) -> p k n", k=4),
                                fr(uhi[:, 4 * m:4 * m + 4, cut]), ALU.subtract).then_inc(at_ready, 1)

            v.wait_ge(att_in, 16)
            maxima(0)
            maxima(1)
            for n in range(UNITS + 1):
                if n + 2 < UNITS:
                    maxima(n + 2)
                if n < UNITS:
                    totals(n)
                if n < 4:
                    preps((110, 111, 114, 115)[n])
                if n % 2 == 0 and n >= 4:
                    out_lo((n - 4) // 2)
                if n:
                    take_out(n - 1)
            out_lo(UNITS // 2 - 1)
            v.wait_ge(resid_in, 16 * T)
            for t in range(T):
                if t == T - 1:
                    preps(112, 113)
                add_out(FIRST["op0"] + t, t, 0, 1.0)
            diagonal(G_F1)
            for t in range(T):
                g = half_group("op1", t)
                add_out(g, t, 1, 1.0)
                v.wait_ge(dve_evac, DVE_BEFORE[g] + 1)
                norm(2, t)
                if t == 4:
                    gate_row_made("gf1")
                    preps(116, 117)
                if t >= LAG:
                    make_lo(TR_LN2, t - LAG)
            for t in range(T - LAG, T):
                make_lo(TR_LN2, t)
            v.wait_ge(h_written, 3 * T)
            with v.Fori(0, end) as i:
                mlp_chunk(FIRST["mlp1"], W_MLP1, LOADS_MLP1, 8 * CHUNKS, i, 8)

            def final(t):
                v.wait_ge(xhat_ready, 3 * T + t + 1)
                tile = resid[:, t, 0:D]
                step.mark(v.tensor_tensor(tile, tile, lnrows[:, 0, :], ALU.mult))
                v.tensor_tensor(tile, tile, lnrows[:, 1, :], ALU.add).then_inc(final_ready, 1)

            def tail_out(t):
                norm(3, t)
                if t >= 1:
                    final(t - 1)

            v.wait_ge(rows_in, 128)
            mlp_chunk(FIRST["mlp1"] + 24 * end, W_MLP1 + 8 * end, LOADS_MLP1 + 8 * end, 8 * CHUNKS + 8 * end,
                      tail=tail_out)
            final(T - 1)

        @block.tensor
        def _(pe):
            def product(dst, left_hi, left_lo, right_hi, right_lo, start, stop):
                pe.matmul(dst, left_hi, right_hi, start=start, stop=False)
                pe.matmul(dst, left_hi, right_lo, start=False, stop=False)
                return pe.matmul(dst, left_lo, right_hi, start=False, stop=stop)

            def need(w):
                pe.wait_ge(loads_used, NUMBER["w", w] + 1)

            def sum_vector(vec, i=0, load=None, per=0):
                pe.wait_ge(loads_used, (NUMBER["ada", vec, K - 1] if load is None else load) + 1 + per * i)
                if vec:
                    pe.wait_ge(sum_read, vec + i)
                for k in range(K):
                    last = pe.matmul(ps[:, M, k:k + 1], acc[:, k * P:(k + 1) * P], ones[:, 0:1], start=True,
                                     stop=True)
                last.then_inc(sum_done, 1)

            def build_row(g, n):
                pe.wait_ge(diag_ready, n)
                for half in range(2):
                    wait_evac(pe, g + half)
                    for k in range(4):
                        last = pe.matmul(ps[:, (g + half) % RING, k * P:(k + 1) * P],
                                         ones[:, 0:1].to_broadcast([P, P]),
                                         acc[:, (4 * half + k) * P:(4 * half + k + 1) * P], start=True, stop=True)
                    last.then_inc(group_done, 1)

            def by_token(g, w0, t, part=(0, 1, 2, 3)):
                for j in part:
                    w = w0 + j
                    if t == 0:
                        need(w)
                    if j == 0:
                        wait_evac(pe, g)
                    s = slot_of(w)
                    for kk in range(2):
                        k = 2 * j + kk
                        cut, col = slice(t * P, (t + 1) * P), slice(kk * HALF, (kk + 1) * HALF)
                        last = product(ps[:, g % RING, :], uhi[:, k, cut], ulo[:, k, cut], whi[:, s, col],
                                       wlo[:, s, col], start=(j == 0 and kk == 0), stop=(j == 3 and kk == 1))
                if part[-1] == 3:
                    last.then_inc(group_done, 1)

            def transpose_tile(event, t, src):
                for j in range(2):
                    n = 2 * (event + t) + j
                    if n >= 4:
                        pe.wait_ge(tr_evac, n - 3)
                    for k in range(4):
                        last = pe.transpose(ps[:, X + n % 4, k * P:(k + 1) * P],
                                            src[:, (4 * j + k) * P:(4 * j + k + 1) * P], ident[:])
                    last.then_inc(tr_done, 1)

            pe.wait_ge(consts_in, 96)
            pe.wait_ge(gate_v, 1)
            sum_vector(SC_M0)
            sum_vector(SH_M0)

            def qk_head(n):
                need(n)
                for half in range(2):
                    g = FIRST["qk"] + 2 * n + half
                    wait_evac(pe, g)
                    cut = slice(half * HALF, (half + 1) * HALF)
                    s = slot_of(n)
                    for k in range(K):
                        if n == 0:
                            pe.wait_ge(u_ready, K * half + k + 1)
                        col = slice(k * P, (k + 1) * P)
                        last = product(ps[:, g % RING, :], whi[:, s, col], wlo[:, s, col], uhi[:, k, cut],
                                       ulo[:, k, cut], start=(k == 0), stop=(k == K - 1))
                    last.then_inc(group_done, 1)

            qk_head(0)
            pe.wait_ge(gate_v, 2)
            pe.wait_ge(sum_read, 2)
            for t in range(T):
                for k in range(K):
                    cut, col = slice(t * P, (t + 1) * P), slice(k * 8, (k + 1) * 8)
                    last = product(ps[:, M, t * 8:(t + 1) * 8], uhi[:, k, cut], ulo[:, k, cut], gwhi[:, col],
                                   gwlo[:, col], start=(k == 0), stop=(k == K - 1))
            last.then_inc(gate_m, 1)
            qk_head(1)
            pe.wait_ge(gate_v, 6)
            for j in range(2):
                last = pe.transpose(ps[0:HC, M, j * P:(j + 1) * P], gt[:, 1, j * HC:(j + 1) * HC], ident[:])
            last.then_inc(gate_m, 1)
            qk_head(2)
            row = scratch[0:HC].rearrange("p a (b n) -> p (a b) n", n=P)
            pe.wait_ge(gate_v, 7)
            for j, r in enumerate((2, 4)):
                last = pe.matmul(ps[0:1, M, j * HC:(j + 1) * HC], row[:, r, P - 1:P], ident[0:HC, 0:HC],
                                 start=True, stop=True)
            last.then_inc(gate_m, 1)
            qk_head(3)
            pe.wait_ge(gate_v, 8)
            pe.matmul(ps[0:HC, M, 0:1], gt[0:1, 2, HC:2 * HC], ones[0:1, 0:1], start=True,
                      stop=True).then_inc(gate_m, 1)
            qk_head(4)
            pe.wait_ge(gate_e, 6)
            for j, src in enumerate((row[:, 3, :], winter[:], row[:, 5, :], row[:, 6, :])):
                pe.transpose(ps[:, M, j * HC:(j + 1) * HC], src, ident[0:HC, 0:HC])
            pe.matmul(ps[:, M, 4 * HC:5 * HC], winter[:, P - 1:P].to_broadcast([HC, P]), ident[0:HC, 0:HC],
                      start=True, stop=True).then_inc(gate_m, 1)
            for n in (5, 6, 7):
                qk_head(n)
            pe.wait_ge(gate_v, 11)
            sum_vector(G_M0)

            for nh in range(2):
                for t in range(T):
                    g = FIRST["v"] + T * nh + t
                    by_token(g, W_V + 4 * nh, t)
                    if nh == 0 and t == 4:
                        sum_vector(SH_F0)
                    if nh == 1 and t == 0:
                        sum_vector(SC_F0)
                    if nh == 1 and t == 4:
                        sum_vector(G_F0)

            def chunk_rows(c, dst, src):
                for h in range(H):
                    r = h * T + c
                    last = pe.matmul(ps[:, dst, h * P:(h + 1) * P], ident[0:HC, r:r + 1].to_broadcast([HC, P]),
                                     src[:], start=True, stop=True)
                last.then_inc(mix, 1)

            pe.wait_ge(act_evac, 16)
            pe.wait_ge(dve_evac, 16)
            for c in range(T):
                if c:
                    pe.wait_ge(c_updated, H * c)
                chunk_rows(c, X, negm)
                chunk_rows(c, X + 3, winter)
                for h in range(H):
                    last = pe.matmul(ps[:, X + 1, h * P:(h + 1) * P], qk[:, c, (H + h) * P:(H + h + 1) * P],
                                     qk[:, c, h * P:(h + 1) * P], start=True, stop=True)
                last.then_inc(mix, 1)
                for h in range(H):
                    last = pe.transpose(ps[:, X + 2, h * P:(h + 1) * P], qk[:, c, (H + h) * P:(H + h + 1) * P],
                                        ident[:])
                last.then_inc(mix, 1)
                if c == 0:
                    sum_vector(SH_KV)
                else:
                    by_token(FIRST["o0"] + c - 1, W_O, c - 1, part=(0, 1))
                pe.wait_ge(s_ready, 2 * c + 2)
                pe.wait_ge(ktok_ready, c + 1)
                for h in range(H):
                    val = resid[:, c, h * (DV + 1):(h + 1) * (DV + 1)]
                    pe.matmul(ps[:, X + h, 0:DV + 1], smat[:, h, :], val, start=True, stop=False)
                    pe.matmul(ps[:, X + h, 0:DV + 1], qk[:, c, h * P:(h + 1) * P], cstate[:, h, :], start=False,
                              stop=True).then_inc(num_done, 1)
                if c:
                    by_token(FIRST["o0"] + c - 1, W_O, c - 1, part=(2, 3))
                if c < T - 1:
                    pe.wait_ge(hs_ready, c + 1)
                    for h in range(H):
                        val = resid[:, c, h * (DV + 1):(h + 1) * (DV + 1)]
                        pe.matmul(ps[:, X + h, 0:DV + 1], ktok[:, h, :], val, start=True,
                                  stop=True).then_inc(state_done, 1)
            by_token(FIRST["o0"] + T - 1, W_O, T - 1)
            pe.wait_ge(hs_ready, T)
            for t in range(T):
                g = o_group(1, t)
                by_token(g, W_O + 4, t)
                if t == 1:
                    build_row(FIRST["gm0"], 1)
                if t >= 1:
                    pe.wait_ge(gated, T + t)
                    transpose_tile(TR_HS, t - 1, qk[:, t - 1, :])
            pe.wait_ge(gated, 2 * T)
            transpose_tile(TR_HS, T - 1, qk[:, T - 1, :])

            for t in range(T):
                pe.wait_ge(ut_ready, 2 * (TR_HS + t) + 2)
                by_token(FIRST["out0"] + t, W_OUT, t)

            def normed(event, ln, t):
                pe.wait_ge(xhat_ready, T * ln + t + 1)
                transpose_tile(event, t, resid[:, t, :])

            def second_half(name, gate, n, w0, ln, event):
                for t in range(T):
                    g = half_group(name, t)
                    by_token(g, w0, t)
                    if t == 3:
                        build_row(FIRST[gate], n)
                    if t >= LAG:
                        normed(event, ln, t - LAG)
                for t in range(T - LAG, T):
                    normed(event, ln, t)

            second_half("out1", "gf0", 2, W_OUT + 4, 0, TR_LN0)

            def mlp_chunk(first, w0, load0, h0, i=0, per=0, with_ada=False, tail=None):
                def up(f):
                    pe.wait_ge(loads_used, load0 + (CHUNK_LOADS.index(f) + 1 if f >= 2 else 0) + per * i)
                    for half in range(2):
                        g = first + 2 * f + half
                        wait_evac(pe, g, i, 16 if ENGINES[g - RING] == "D" else 8)
                        cut = slice(half * HALF, (half + 1) * HALF)
                        for k in range(K):
                            col = slice(k * P, (k + 1) * P)
                            last = product(ps[:, g % RING, :], whi[:, f % 2, col], wlo[:, f % 2, col],
                                           uhi[:, k, cut], ulo[:, k, cut], start=(k == 0), stop=(k == K - 1))
                        last.then_inc(group_done, 1)

                for f in range(4):
                    up(f)
                pe.wait_ge(loads_used, load0 + CHUNK_LOADS.index(7) + 1 + per * i)
                for d in range(16):
                    t, nh = d // 2, d % 2
                    g = first + 8 + d
                    if d in (0, 8):
                        pe.wait_ge(h_ready, h0 + 7 + d // 8 + 8 * i)
                    wait_evac(pe, g, i, 16 if ENGINES[g - RING] == "D" else 8)
                    cut, col = slice(t * P, (t + 1) * P), slice(nh * HALF, (nh + 1) * HALF)
                    for f in range(4):
                        last = product(ps[:, g % RING, :], hhi[:, f, cut], hlo[:, f, cut], whi[:, 2 + f, col],
                                       wlo[:, 2 + f, col], start=(f == 0), stop=(f == 3))
                    last.then_inc(group_done, 1)
                    if with_ada and d == 11:
                        sum_vector(SC_KV, i, load0 + 15, per)
                    if tail and nh == 1 and t >= LAG:
                        tail(t - LAG)

            pe.wait_ge(ut_ready, 2 * (TR_LN0 + T))
            end = CHUNKS - 1
            with pe.Fori(0, end) as i:
                mlp_chunk(FIRST["mlp0"], W_MLP0, LOADS_MLP0, 0, i, 16, with_ada=True)
            mlp_chunk(FIRST["mlp0"] + 24 * end, W_MLP0 + 8 * end, LOADS_MLP0 + 16 * end, 8 * end,
                      tail=lambda t: normed(TR_KV, 1, t))
            normed(TR_KV, 1, T - 2)

            def k_transposed(t):
                pe.wait_ge(roped, t + 1)
                if t:
                    pe.wait_ge(kt_evac, t)
                else:
                    pe.wait_ge(sum_read, NVEC)
                for m in range(2):
                    last = pe.transpose(ps[:, M, m * P:(m + 1) * P], probs[:, t % 2, 0, m * P:(m + 1) * P], ident[:])
                last.then_inc(kt_done, 1)

            def q_input(t):
                pe.wait_ge(h_written, T + t + 1)
                transpose_tile(TR_Q, t, resid[:, t, :])

            for t in range(T):
                pe.wait_ge(ut_ready, 2 * (TR_KV + t) + 2)
                by_token(kv_group(t), W_KV, t)
                if t == 0:
                    normed(TR_KV, 1, T - 1)
                if t == 2:
                    build_row(FIRST["gm1"], 3)
                if t >= 1:
                    k_transposed(t - 1)
                    q_input(t - 1)
            k_transposed(T - 1)
            q_input(T - 1)
            for nh in range(2):
                for t in range(T):
                    pe.wait_ge(ut_ready, 2 * (TR_Q + t) + 2)
                    g = FIRST["q"] + T * nh + t
                    by_token(g, W_Q + 4 * nh, t)

            def side_turn(event):
                kind, pair = event
                if SIDE.index(event):
                    before, count = SIDE[SIDE.index(event) - 1]
                    pe.wait_ge(q_taken if before == "q" else at_ready, count + 1)
                if kind == "o":
                    pe.wait_ge(out_ready, 2 * pair + 2)
                for j in range(4):
                    last = pe.transpose(ps[:, X + 3, j * P:(j + 1) * P],
                                        resid[:, pair // 2, (4 * (pair % 2) + j) * P:(4 * (pair % 2) + j + 1) * P],
                                        ident[:])
                last.then_inc(side_t, 1)

            def side(n):
                if n % 2 == 1 and (n + 3) // 2 < UNITS // 2:
                    side_turn(("q", (n + 3) // 2))
                if n % 2 == 0 and n >= 4:
                    side_turn(("o", (n - 4) // 2))

            def make_scores(n):
                b, u = n // 4, n % 4
                lo = P if b == 0 else 0
                m, part = u // 2, slice(u % 2 * HD, (u % 2 + 1) * HD)
                pe.wait_ge(q_taken, n // 2 + 1)
                if n >= 2:
                    pe.wait_ge(max_ready, n - 1)
                for g in range(GROUP):
                    bank, at = 2 * (n % 2) + g // 2, g % 2 * 2 * P
                    last = pe.matmul(ps[:, bank, at + lo:at + 2 * P], acc[part, (4 * m + g) * P:(4 * m + g + 1) * P],
                                     kt[part, m, (b - 1) * P + lo:(b + 1) * P], start=True, stop=True)
                last.then_inc(scores, 1)

            def turn_p(n):
                pe.wait_ge(exp_ready, n + 1)
                if n:
                    pe.wait_ge(p_taken, n)
                for j in range(1 if n < 4 else 0, 2):
                    for g in range(GROUP):
                        last = pe.transpose(ps[:, X + j, g * P:(g + 1) * P],
                                            probs[:, n % 3, g, j * P:(j + 1) * P], ident[:])
                last.then_inc(p_t, 1)

            def make_pv(n):
                b, u = n // 4, n % 4
                pe.wait_ge(p_taken, n + 1)
                if n:
                    pe.wait_ge(out_ready, n)
                first = 1 if b == 0 else 0
                for g in range(GROUP):
                    for j in range(first, 2):
                        last = pe.matmul(ps[:, X + 2, g * HD:(g + 1) * HD], probst[:, n % 2, j, g * P:(g + 1) * P],
                                         vv[:, b - 1 + j, u * HD:(u + 1) * HD], start=(j == first), stop=(j == 1))
                last.then_inc(pv_done, 1)

            pe.wait_ge(roped, 3 * T)
            pe.wait_ge(kt_evac, T)
            pe.wait_ge(ut_ready, 2 * (TR_Q + T))
            side_turn(("q", 0))
            make_scores(0)
            make_scores(1)
            side_turn(("q", 1))
            for n in range(UNITS + 1):
                if n + 2 < UNITS:
                    make_scores(n + 2)
                if n < UNITS:
                    turn_p(n)
                side(n)
                if n:
                    make_pv(n - 1)
            side_turn(("o", UNITS // 2 - 1))
            pe.wait_ge(at_ready, 2 * T)
            for t in range(T):
                by_token(FIRST["op0"] + t, W_OP, t)
            second_half("op1", "gf1", 4, W_OP + 4, 2, TR_LN2)
            pe.wait_ge(ut_ready, 2 * (TR_LN2 + T))
            with pe.Fori(0, end) as i:
                mlp_chunk(FIRST["mlp1"], W_MLP1, LOADS_MLP1, 8 * CHUNKS, i, 8)
            mlp_chunk(FIRST["mlp1"] + 24 * end, W_MLP1 + 8 * end, LOADS_MLP1 + 8 * end, 8 * CHUNKS + 8 * end)


def arrange(inputs):
    f = {k: np.asarray(a) for k, a in inputs.items()}
    ada = [f["ada_w"][0].reshape(K, P, 6, D), f["kv_ada_w"].reshape(K, P, 2, D), f["ada_w"][1].reshape(K, P, 6, D)]
    bias = [f["ada_b"][0].reshape(6, D), f["kv_ada_b"].reshape(2, D), f["ada_b"][1].reshape(6, D)]
    where = [(0, 1), (0, 0), (0, 2), (0, 3), (0, 4), (0, 5), (1, 0), (1, 1), (2, 0), (2, 1), (2, 2), (2, 3), (2, 4),
             (2, 5)]

    def by_feature(rows):
        return np.ascontiguousarray(np.stack(rows).reshape(len(rows), K, P).transpose(2, 0, 1))

    def up_blocks(w):
        n = w.shape[1] // P
        return w.reshape(K, P, n, P).transpose(2, 1, 0, 3).reshape(n, P, D)

    def half_blocks(w):
        n = w.shape[1] // HALF
        return w.reshape(4, 2, P, n, HALF).transpose(3, 0, 2, 1, 4).reshape(4 * n, P, D)

    a_in, nq = f["a_w_in"][0], H * P
    blocks = [up_blocks(a_in[:, 0:2 * nq]), half_blocks(a_in[:, 2 * nq:2 * nq + D]),
              half_blocks(a_in[:, 2 * nq + D:2 * nq + 2 * D]), half_blocks(f["a_w_out"][0])]
    w_q = f["b_w_q"][0].reshape(D, 2, 2, GROUP, HD).transpose(0, 1, 3, 2, 4).reshape(D, D)
    for layer in range(2):
        up, down = up_blocks(f["mlp_w_up"][layer]), f["mlp_w_down"][layer].reshape(DFF // P, P, D)
        blocks.append(np.stack([up.reshape(CHUNKS, 4, P, D), down.reshape(CHUNKS, 4, P, D)], 1).reshape(-1, P, D))
        if layer == 0:
            blocks += [half_blocks(f["w_kv"]), half_blocks(w_q), half_blocks(f["b_w_o"][0])]
    blocks = np.concatenate(blocks)
    stream = np.empty((N_LOADS, P, D), np.float32)
    for n, x in enumerate(ORDER):
        stream[n] = blocks[x[1]] if x[0] == "w" else ada[where[x[1]][0]][x[2], :, where[x[1]][1]]
    j = np.arange(2 * P)[None, :]
    i = np.arange(P)[:, None]
    return {
        "stream": stream,
        "xt": np.ascontiguousarray(f["x"][0].T).reshape(K, P, S),
        "x": np.ascontiguousarray(f["x"][0]),
        "ident": np.eye(P, dtype=np.float32),
        "mod_bias": by_feature([bias[m][r] for m, r in where]),
        "fcols": by_feature([*f["ln_g"][0:3], *f["ln_b"][0:3], f["a_norm_w"][0]]),
        "c": np.ascontiguousarray(f["c"][0].reshape(K, P).T),
        "gate_w": np.ascontiguousarray(a_in[:, 2 * nq + 2 * D:].reshape(K, P, 8).transpose(1, 0, 2).reshape(P, K * 8)),
        "gate_b": np.repeat(f["a_b_gates"][0], T),
        "ln_g": np.ascontiguousarray(f["ln_g"]),
        "ln_b": np.ascontiguousarray(f["ln_b"]),
        "sinks": np.ascontiguousarray(f["b_sinks"][0]),
        "positions": np.ascontiguousarray(f["positions"][0].reshape(T, P).T),
        "inv_freq": (np.float32(THETA) ** (-np.arange(RH, dtype=np.float32) / np.float32(RH))).astype(np.float32),
        "mask": np.where((j > i) & (j <= i + P), 0.0, MASKED).astype(np.float32),
    }


def kernel(**inputs):
    import concourse.bacc as bacc
    from concourse.bass_utils import run_bass_kernel_spmd

    nc = bacc.Bacc("TRN2", target_bir_lowering=False, num_devices=1)
    arrays = {"in_" + k: a for k, a in arrange(inputs).items()}
    aps = {k[3:]: nc.dram_tensor(k, a.shape, mybir.dt.from_np(a.dtype), kind="ExternalInput").ap()
           for k, a in arrays.items()}
    out = nc.dram_tensor("out", (S, D), F32, kind="ExternalOutput").ap()
    build(nc, aps.pop("stream"), aps.pop("xt"), aps.pop("x"), aps, out)
    result = run_bass_kernel_spmd(nc, [arrays], core_ids=[0])
    return result.results[0]["out"].reshape(1, S, D)
```

```python
import math
from contextlib import ExitStack

import numpy as np
import concourse.bass as bass
from concourse import mybir

F32 = mybir.dt.float32
F32R = mybir.dt.float32r
I32 = mybir.dt.int32
ALU = mybir.AluOpType
ACT = mybir.ActivationFunctionType

P = 128
S = 1024
D = 1024
DFF = 4 * D
T = S // P
K = D // P
HALF = 512
H = 4
DV = D // H
HC = H * T
AH = 16
UNITS = AH // 4 * T
HD = 64
GROUP = 4
ROT = HD // 4
RH = ROT // 2
THETA = 500000.0
CAP = 15.0
ALPHA = 4.0 ** 0.25
LN_EPS = 1e-5
RMS_EPS = 1e-6
MASKED = -3.0e38
ROUNDER = 1.5 * 2.0 ** 23
TWO_PI = (6.28125, 1.9350051879882812e-3, 3.0199159819733e-7)
PI_IN = 3.1415925

SC_M0, SH_M0, G_M0, SH_F0, SC_F0, G_F0, SH_KV, SC_KV, SH_M1, SC_M1, G_M1, SH_F1, SC_F1, G_F1 = range(14)
NVEC = 14

W_QK, W_V, W_O, W_OUT, W_MLP0 = 0, 8, 16, 24, 32
CHUNKS = DFF // HALF
W_KV = W_MLP0 + 8 * CHUNKS
W_Q = W_KV + 4
W_OP = W_Q + 8
W_MLP1 = W_OP + 8
N_W = W_MLP1 + 8 * CHUNKS

SLOTS = 6
RING = 3


def slot_of(w):
    for first in (W_MLP0, W_MLP1):
        if first <= w < first + 8 * CHUNKS:
            j = (w - first) % 8
            return j % 2 if j < 4 else j - 2
    if w < W_MLP0:
        return (w - W_MLP0) % SLOTS
    if w < W_OP:
        return (w - W_KV) % SLOTS
    return [0, 1, 2, 3, 2, 3, 4, 5][w - W_OP]


def former_in_slot(w):
    for first in (W_MLP0, W_MLP1):
        if first <= w < first + 8 * CHUNKS:
            j = (w - first) % 8
            if j >= 2 and (w >= first + 8 or j < 4):
                return w - (2 if j < 4 else 8)
            if w >= first + 8:
                return w - 6
    before = [x for x in range(w) if slot_of(x) == slot_of(w)]
    return before[-1] if before else None


def is_scaled(w):
    if W_OUT <= w < W_MLP0 or W_OP <= w < W_MLP1:
        return True
    return any(f <= w < f + 8 * CHUNKS and (w - f) % 8 >= 4 for f in (W_MLP0, W_MLP1))


CHUNK_LOADS = [4, 5, 2, 3, 6, 7, 8, 9]
UP = [(0, 0), (1, 0), (0, 1), (1, 1), (2, 0), (3, 0), (2, 1), (3, 1)]


def load_order():
    out = []

    def ada(v, ks=range(K)):
        out.extend(("ada", v, k) for k in ks)

    def w(*blocks):
        out.extend(("w", b) for b in blocks)

    w(0, 1, 2, 3, 4, 5, 6, 7, 8)
    ada(G_M0, range(2))
    w(9)
    ada(G_M0, range(2, 4))
    w(10)
    ada(G_M0, range(4, 8))
    w(11, 12, 13)
    ada(SH_F0)
    w(14, 15)
    for t in range(T):
        ada(SC_F0, range(t, t + 1))
        if t in (1, 2):
            w(15 + t)
    w(18, 19)
    ada(G_F0, range(2))
    w(20, 21)
    ada(G_F0, range(2, K)), ada(SH_KV)
    w(22, 23, 24, 25, 26, 27, 28, 29, 30, 31, 32, 33)
    for c in range(CHUNKS):
        w(*[W_MLP0 + 8 * c + j for j in CHUNK_LOADS])
        if c < CHUNKS - 1:
            ada(SC_KV + c)
    w(98, 99, 100, 101, 102, 103, 104, 105, 106, 107, 108, 109, 110, 111, 114, 115, 112, 113, 116, 117)
    for c in range(CHUNKS):
        w(*[W_MLP1 + 8 * c + j for j in CHUNK_LOADS if W_MLP1 + 8 * c + j < N_W])
    return out


ORDER = load_order()
NUMBER = {x: n for n, x in enumerate(ORDER)}
LOADS_MLP0, LOADS_MLP1 = NUMBER["w", W_MLP0 + 4], NUMBER["w", W_MLP1 + 4]
N_LOADS = len(ORDER)
WEIGHTS_BEFORE = [sum(x[0] == "w" for x in ORDER[:n]) for n in range(N_LOADS + 1)]
SCALED_BEFORE = [sum(x[0] == "w" and is_scaled(x[1]) for x in ORDER[:n]) for n in range(N_LOADS + 1)]
assert sorted(x[1] for x in ORDER if x[0] == "w") == list(range(N_W))


def group_engines():
    out, first = "", {}

    def add(name, what):
        nonlocal out
        first[name] = len(out)
        out += what

    add("qk", "A" * 16)
    add("v", "D" * 16)
    add("o0", "A" * 8)
    add("o1a", "A" * 2)
    add("gm0", "A" * 2)
    add("o1b", "A" * 6)
    add("out0", "D" * 8)
    add("out1a", "D" * 4)
    add("gf0", "A" * 2)
    add("out1b", "D" * 4)
    add("mlp0", ("A" * 8 + "D" * 16) * CHUNKS)
    add("kva", "D" * 3)
    add("gm1", "A" * 2)
    add("kvb", "D" * 5)
    add("q", "D" * 16)
    add("op0", "D" * 8)
    add("op1a", "D" * 4)
    add("gf1", "A" * 2)
    add("op1b", "D" * 4)
    add("mlp1", ("A" * 8 + "D" * 16) * CHUNKS)
    return out, first


ENGINES, FIRST = group_engines()
ACT_BEFORE = [ENGINES[:g].count("A") for g in range(len(ENGINES) + 1)]
DVE_BEFORE = [ENGINES[:g].count("D") for g in range(len(ENGINES) + 1)]

PASSES = [W_V, W_V + 4, W_O, W_O + 4, W_OUT, W_OUT + 4, W_KV, W_Q, W_Q + 4, W_OP, W_OP + 4]


def early_release(w):
    for n, first in enumerate(PASSES):
        if first <= w < first + 3:
            return 3 * n + w - first + 1
    return None


def groups_through(w):
    for first, name in ((W_MLP0, "mlp0"), (W_MLP1, "mlp1")):
        if first <= w < first + 8 * CHUNKS:
            c, j = divmod(w - first, 8)
            return FIRST[name] + 24 * c + (UP.index((j, 1)) + 1 if j < 4 else 24)
    if w < W_V:
        return FIRST["qk"] + 2 * w + 2
    for first, names in ((W_OP, ("op0", "op1b")), (W_Q, ("q", "q")), (W_KV, ("kvb", "kvb")), (W_OUT, ("out0", "out1b")),
                         (W_O, ("o0", "o1b")), (W_V, ("v", "v"))):
        if w >= first:
            second = (w - first) // 4
            size = {"q": T * (1 + second), "v": T * (1 + second), "kvb": 5, "o1b": 6, "out1b": 4, "op1b": 4}
            return FIRST[names[second]] + size.get(names[second], T)


TR_HS, TR_LN0, TR_KV, TR_Q, TR_LN2 = (T * i for i in range(5))


LAG, LAG_H = 2, 4


def build(nc, stream, early, xt, x, consts, out):
    ctx = ExitStack()

    def sb(name, shape, dt=F32, where=ctx):
        return where.enter_context(nc.sbuf_tensor(name, shape, dt))

    def sem(name):
        return ctx.enter_context(nc.semaphore(name))

    with ctx:
        resid = sb("resid", [P, T, H * (DV + 1)])
        with ExitStack() as a:
            early_place = sb("early_place", [P, 8 * D], where=a)
            u_whole = sb("u_whole", [P, K, S], where=a)
        uhi = sb("uhi", [P, K, S], F32R)
        ulo = sb("ulo", [P, K, S], F32R)
        whi = sb("whi", [P, SLOTS, D], F32R)
        wlo = sb("wlo", [P, SLOTS, D], F32R)
        stage = sb("stage", [P, 2, D])
        scratch = sb("scratch", [P, 2, HALF])
        acc = sb("acc", [P, D])
        mods = sb("mods", [P, NVEC, K])
        mulv = sb("mulv", [P, 5, K])
        addv = sb("addv", [P, 5, K])
        fcols = sb("fcols", [P, 7, K])
        ident = sb("ident", [P, P])
        ones = sb("ones", [P, 1])
        cs = sb("cs", [P, 2, K])
        pair_sum = sb("pair_sum", [16, 8])
        stats = sb("stats", [P, 2, 12])
        moments = sb("moments", [P, 2, 2])
        neghalf = sb("neghalf", [P, H])
        rstd = sb("rstd", [P, 2, 1])
        nmr = sb("nmr", [P, 2, 1])
        sumsq, factor, mean = stats[:, 1, 4:4 + H], stats[:, 1, 0:H], stats[:, 0, H:2 * H]

        with ExitStack() as a:
            cstate = sb("cstate", [P, H, DV + 1], where=a)
        gate_row = sb("gate_row", [P, H * (DV + 1)])
        with ExitStack() as a:
            negm = sb("negm", [HC, P], where=a)
            winter = sb("winter", [HC, P], where=a)
            cols = sb("cols", [P, 5, HC], where=a)
        with ExitStack() as a:
            rope = sb("rope", [P, T, 2 * ROT], where=a)
            angle = sb("angle", [P, T, RH], where=a)
            turns = sb("turns", [P, T, RH], where=a)
            sinks = sb("sinks", [P, AH], where=a)
            posi = sb("posi", [P, T], I32, where=a)
        small = sb("small", [P, 416])
        with ExitStack() as a:
            dmat = sb("dmat", [P, H, P], where=a)
            smat = sb("smat", [P, H, P], where=a)
            ktok = sb("ktok", [P, H, P], where=a)
            gw = sb("gw", [P, K, 8], where=a)
            gws = sb("gws", [P, K, 16], F32R, where=a)
            gt = sb("gt", [P, 4, 2 * HC], where=a)
        m_prev_col = gt[0:HC, 3, 0:1]
        with ExitStack() as a:
            probst = sb("probst", [P, 2, 2, HALF], where=a)
        lnrows = sb("lnrows", [P, 2, D])
        with ExitStack() as a:
            qk = sb("qk", [P, T, D], where=a)
        with ExitStack() as a:
            hhi = sb("hhi", [P, 4, S], F32R, where=a)
            with ExitStack() as b:
                h_whole = sb("h_whole", [P, 4, S], where=b)
            hlo = sb("hlo", [P, 4, S], F32R, where=a)
        with ExitStack() as a:
            kt = sb("kt", [P, 2, S], where=a)
            vv = sb("vv", [P, T, 4 * HD], where=a)
            probs = sb("probs", [P, 3, GROUP, 2 * P], where=a)
            mask = sb("mask", [P, 2 * P], where=a)
            rtmp = sb("rtmp", [P, 2, 8, ROT], where=a)
            att = sb("att", [P, 3, 6, GROUP], where=a)
        aux = sb("aux", [P, 8 * D])
        ps = ctx.enter_context(nc.psum_tensor("ps", [P, 8, HALF], F32))
        M = RING
        X = RING + 1
        resid_dram = nc.dram_tensor("resid_dram", (T, P, D), F32, kind="Internal").ap()

        stage_loaded = [sem("stage_loaded0"), sem("stage_loaded1")]
        early_in = [sem(f"early_in{g}") for g in range(4)]
        early_sum = sem("early_sum")
        loads_used = sem("loads_used")
        scaled = sem("scaled")
        hi_ready = sem("hi_ready")
        released = sem("released")
        group_done = sem("group_done")
        act_evac = sem("act_evac")
        dve_evac = sem("dve_evac")
        consts_in = sem("consts_in")
        c_in = sem("c_in")
        xt_in = sem("xt_in")
        dve_step = sem("dve_step")
        pool_step = sem("pool_step")
        sum_done = sem("sum_done")
        sum_read = sem("sum_read")
        gate_m = sem("gate_m")
        u_made = sem("u_made")
        u_hi = sem("u_hi")
        u_ready = sem("u_ready")
        gate_e = sem("gate_e")
        gate_v = sem("gate_v")
        diag_ready = sem("diag_ready")
        mix = sem("mix")
        d_ready = sem("d_ready")
        d_masked = sem("d_masked")
        s_ready = sem("s_ready")
        ktok_ready = sem("ktok_ready")
        num_done = sem("num_done")
        ss_ready = sem("ss_ready")
        ms_ready = sem("ms_ready")
        rms_ready = sem("rms_ready")
        f_ready = sem("f_ready")
        hs_ready = sem("hs_ready")
        state_done = sem("state_done")
        c_updated = sem("c_updated")
        gated = sem("gated")
        x_in = sem("x_in")
        tr_done = sem("tr_done")
        tr_taken = [sem("tr_taken0"), sem("tr_taken1")]
        ut_hi = sem("ut_hi")
        ut_ready = sem("ut_ready")
        moments_ready = sem("moments_ready")
        ln_ready = sem("ln_ready")
        xhat_ready = sem("xhat_ready")
        rows_in = sem("rows_in")
        h_written = sem("h_written")
        relu_sq = sem("relu_sq")
        h_hi = sem("h_hi")
        h_ready = sem("h_ready")
        rope_in = sem("rope_in")
        angle_ready = sem("angle_ready")
        sin_ready = sem("sin_ready")
        att_in = sem("att_in")
        spilled = sem("spilled")
        roped = sem("roped")
        kt_done = sem("kt_done")
        kt_evac = sem("kt_evac")
        side_t = sem("side_t")
        q_taken = sem("q_taken")
        p_t = sem("p_t")
        p_taken = sem("p_taken")
        scores = sem("scores")
        max_ready = sem("max_ready")
        exp_ready = sem("exp_ready")
        pv_done = sem("pv_done")
        out_ready = sem("out_ready")
        at_hi = sem("at_hi")
        at_ready = sem("at_ready")
        resid_in = sem("resid_in")
        final_ready = sem("final_ready")
        stored = sem("stored")

        def fr(ap):
            return ap.bitcast(F32)

        def early_blocks(g):
            place = aux[:] if g < 2 else early_place[:]
            return place[:, g % 2 * 4 * D:(g % 2 + 1) * 4 * D]

        class Steps:

            def __init__(self, eng, s):
                self.eng, self.sem, self.n = eng, s, 0

            def mark(self, ins):
                ins.then_inc(self.sem, 1)
                self.n += 1
                self.eng.wait_ge(self.sem, self.n)

        def wait_evac(eng, g, i=0, per=0):
            if g < RING:
                return
            before = g - RING
            count, s = (ACT_BEFORE, act_evac) if ENGINES[before] == "A" else (DVE_BEFORE, dve_evac)
            eng.wait_ge(s, count[before] + 1 + per * i)

        def o_group(nh, t):
            return FIRST["o0"] + t if nh == 0 else FIRST["o1a" if t < 2 else "o1b"] + t - (0 if t < 2 else 2)

        def half_group(name, t):
            return FIRST[name + "a"] + t if t < 4 else FIRST[name + "b"] + t - 4

        def kv_group(t):
            return FIRST["kva"] + t if t < 3 else FIRST["kvb"] + t - 3

        def gate_tanh(nh, t):
            if nh == 0:
                return scratch[:, t % 2, :]
            return (dmat if t % 2 == 0 else smat)[:].rearrange("p h n -> p (h n)")

        SIDE = [("q", 0), ("q", 1)]
        for n in range(UNITS + 1):
            if n % 2 == 1 and (n + 3) // 2 < UNITS // 2:
                SIDE.append(("q", (n + 3) // 2))
            if n % 2 == 0 and n >= 4:
                SIDE.append(("o", (n - 4) // 2))
        SIDE.append(("o", UNITS // 2 - 1))

        def loaded(eng, n, i=0, per=0):
            eng.wait_ge(stage_loaded[n % 2], 16 * (n // 2 + 1) + 8 * per * i)

        block = ctx.enter_context(nc.Block())

        @block.sync
        def _(sp):
            sp.dma_start(cs[:, 0, :], consts["c"]).then_inc(c_in, 16)
            for g in range(4):
                sp.dma_start(early_blocks(g), early[g]).then_inc(early_in[g], 16)
            for k in range(K):
                sp.dma_start(resid[:, k, 0:S], xt[k]).then_inc(xt_in, 16)
            for n in range(2):
                sp.dma_start(stage[:, n, :], stream[n]).then_inc(stage_loaded[n], 16)
            with sp.Fori(1, N_LOADS // 2) as i:
                for b in range(2):
                    sp.wait_ge(loads_used, 2 * i + (b - 1))
                    sp.dma_start(stage[:, b, :], stream[2 * i + b]).then_inc(stage_loaded[b], 16)
            for t in range(T):
                sp.wait_ge(final_ready, t + 1)
                sp.dma_start(out[t * P:(t + 1) * P, :], resid[:, t, 0:D]).then_inc(stored, 16)
            sp.wait_ge(stored, 16 * T)

        @block.gpsimd
        def _(pool):
            step = Steps(pool, pool_step)
            step.mark(pool.memset(neghalf[:], -0.5))
            for c in range(T):
                pool.wait_ge(d_ready, c + 1)
                pool.affine_select(out=dmat[:], in_=dmat[:], compare_op=ALU.is_ge, fill=0.0, base=0,
                                   pattern=[[0, H], [1, P]], channel_multiplier=-1).then_inc(d_masked, 1)
                pool.wait_ge(ms_ready, c + 1)
                pool.tensor_tensor(mean, mean, neghalf[:], ALU.pow).then_inc(rms_ready, 1)
            pool.wait_ge(num_done, H * T)
            pool.wait_ge(state_done, H * (T - 1))
            for t in range(T):
                pool.dma_start(resid[:, t, 0:D], x[t * P:(t + 1) * P, :]).then_inc(x_in, 16)

            def rows(j, scale):
                for r, src in enumerate(("ln_g", "ln_b")):
                    pool.dma_start(lnrows[:, r, :], consts[src][j].partition_broadcast(P)).then_inc(rows_in, 16)
                if scale:
                    pool.wait_ge(rows_in, 32 * (j + 1))
                    step.mark(pool.tensor_scalar(lnrows[:], lnrows[:], ALPHA, None, ALU.mult))

            def norm_scale(ln, t):
                j = t % 2
                pool.wait_ge(moments_ready, T * ln + t + 1)
                step.mark(pool.tensor_scalar(rstd[:, j, :], moments[:, j, 1:2], LN_EPS, None, ALU.add))
                step.mark(pool.tensor_tensor(rstd[:, j, :], rstd[:, j, :], neghalf[:, 0:1], ALU.pow))
                pool.tensor_scalar(nmr[:, j, :], moments[:, j, 0:1], -1.0, rstd[:, j, :], ALU.mult,
                                   ALU.mult).then_inc(ln_ready, 1)

            def write_h(t, event):
                pool.wait_ge(tr_done, 2 * (event + t) + 2)
                step.mark(pool.tensor_tensor(resid[:, t, 0:D], resid[:, t, 0:D], lnrows[:, 0, :], ALU.mult))
                pool.tensor_tensor(resid[:, t, 0:D], resid[:, t, 0:D], lnrows[:, 1, :],
                                   ALU.add).then_inc(h_written, 1)

            pool.wait_ge(hs_ready, H * T)
            pool.dma_start(sinks[:], consts["sinks"].partition_broadcast(P)).then_inc(rope_in, 16)
            pool.dma_start(posi[:], consts["positions"]).then_inc(rope_in, 16)
            pool.dma_start(turns[:, 0, :], consts["inv_freq"].partition_broadcast(P)).then_inc(rope_in, 16)
            pool.wait_ge(gated, 2 * T)
            rows(0, True)
            for t in range(T + LAG_H):
                if t < T:
                    norm_scale(0, t)
                if t >= LAG_H:
                    write_h(t - LAG_H, TR_LN0)
            pool.wait_ge(h_written, T)
            rows(1, True)
            for t in range(T + LAG_H):
                if t < T:
                    norm_scale(1, t)
                if t >= LAG_H:
                    write_h(t - LAG_H, TR_KV)
                    pool.wait_ge(h_written, T + t - LAG_H + 1)
                    pool.dma_start(resid_dram[t - LAG_H], resid[:, t - LAG_H, 0:D]).then_inc(spilled, 16)
            pool.wait_ge(group_done, FIRST["kva"])
            pool.dma_start(mask[:], consts["mask"]).then_inc(att_in, 16)
            for t in range(T):
                pool.wait_ge(side_t, SIDE.index(("o", 2 * t + 1)) + 1)
                pool.dma_start(resid[:, t, 0:D], resid_dram[t]).then_inc(resid_in, 16)
            pool.wait_ge(pv_done, UNITS)
            rows(2, True)
            for t in range(T + LAG_H):
                if t < T:
                    norm_scale(2, t)
                if t >= LAG_H:
                    write_h(t - LAG_H, TR_LN2)
            pool.wait_ge(h_written, 3 * T)
            rows(3, False)
            for t in range(T):
                norm_scale(3, t)

        @block.scalar
        def _(act):
            for dst, name in ((ident[:], "ident"), (mods[:], "mod_bias"), (fcols[:], "fcols"),
                              (pair_sum[:], "pair_sum"), (gw[:], "gate_w")):
                act.dma_start(dst, consts[name]).then_inc(consts_in, 16)
            act.dma_start(gt[:, 0, :], consts["gate_b"].partition_broadcast(P)).then_inc(consts_in, 16)
            act.wait_ge(c_in, 16)
            act.activation(cs[:, 1, :], cs[:, 0, :], ACT.Exp, scale=-1.0).then_inc(gate_e, 1)
            act.wait_ge(consts_in, 96)
            act.activation(gws[:, :, 0:8], gw[:], ACT.Copy).then_inc(gate_e, 1)

            def split(n, w, i=0, per=0):
                if is_scaled(w):
                    act.wait_ge(scaled, SCALED_BEFORE[n] + 1 + 4 * i)
                else:
                    loaded(act, n, i, per)
                former = former_in_slot(w)
                if former is not None:
                    if early_release(former):
                        act.wait_ge(released, early_release(former))
                    else:
                        act.wait_ge(group_done, groups_through(former) + 24 * i)
                act.activation(whi[:, slot_of(w), :], stage[:, n % 2, :], ACT.Copy).then_inc(hi_ready, 1)

            def splits(*blocks):
                for w in blocks:
                    split(NUMBER["w", w], w)

            def first_u(half):
                cut = slice(half * HALF, (half + 1) * HALF)
                for k in range(K):
                    act.wait_ge(u_made, K * half + k + 1)
                    act.activation(uhi[:, k, cut], resid[:, k, cut], ACT.Copy).then_inc(u_hi, 1)

            splits(0)
            first_u(0)
            first_u(1)
            splits(1, 2, 3, 4, 5)

            def evac_qk(n):
                for half in range(2):
                    g = FIRST["qk"] + 2 * n + half
                    act.wait_ge(group_done, g + 1)
                    act.activation(qk[:, 4 * half:4 * half + 4, n * P:(n + 1) * P],
                                   ps[:, g % RING, :].rearrange("p (c t) -> p c t", c=4), ACT.Copy,
                                   scale=1.0 if n < H else 1.0 / math.sqrt(P)).then_inc(act_evac, 1)

            evac_qk(0)
            splits(6)
            act.wait_ge(gate_m, 1)
            act.activation(scratch[0:16], ps[0:16, X:X + 2, :], ACT.Copy).then_inc(gate_e, 1)
            evac_qk(1)
            act.wait_ge(gate_v, 3)
            act.activation(gt[:, 2, :], gt[:, 1, :], ACT.Tanh, scale=1.0 / CAP).then_inc(gate_e, 1)
            act.wait_ge(gate_v, 4)
            act.activation(gt[:, 2, 0:HC], gt[:, 1, HC:2 * HC], ACT.Exp, scale=-1.0).then_inc(gate_e, 1)
            act.wait_ge(gate_v, 5)
            act.activation(gt[:, 3, 0:HC], gt[:, 2, HC:2 * HC], ACT.Ln).then_inc(gate_e, 1)
            splits(7)
            evac_qk(2)
            splits(8)
            evac_qk(3)
            splits(9)
            evac_qk(4)
            splits(10)
            row = scratch[0:HC].rearrange("p a (b n) -> p (a b) n", n=P)
            act.wait_ge(gate_v, 10)
            act.activation(winter[:], row[:, 4, :], ACT.Exp, scale=-1.0, bias=m_prev_col)
            act.activation(row[:, 5, :], row[:, 3, :], ACT.Exp, bias=negm[:, P - 1:P])
            act.activation(row[:, 6, :], row[:, 7, :], ACT.Exp, scale=-1.0).then_inc(gate_e, 1)
            for n, w in ((5, 11), (6, 12), (7, 13)):
                evac_qk(n)
                splits(w)
            splits(14, 15, 16, 17, 18, 19)

            def evac_o(nh, t):
                act.wait_ge(group_done, o_group(nh, t) + 1)
                if t >= 2:
                    act.wait_ge(gated, T * nh + t - 1)
                act.activation(gate_tanh(nh, t), ps[:, o_group(nh, t) % RING, :], ACT.Tanh,
                               scale=0.5).then_inc(act_evac, 1)

            for c in range(T):
                act.wait_ge(mix, 4 * c + 1)
                for h in range(H):
                    last = act.activation(dmat[:, h, :], ps[:, X, h * P:(h + 1) * P], ACT.Exp,
                                          bias=cols[:, 0, h * T + c:h * T + c + 1])
                last.then_inc(d_ready, 1)
                act.wait_ge(mix, 4 * c + 3)
                for h in range(H):
                    last = act.activation(ktok[:, h, :], ps[:, X + 2, h * P:(h + 1) * P], ACT.Copy,
                                          scale=cols[:, 2, h * T + c:h * T + c + 1])
                last.then_inc(ktok_ready, 1)
                act.wait_ge(s_ready, 2 * c + 2)
                for h in range(H):
                    act.wait_ge(num_done, H * c + h + 1)
                    if h >= 2:
                        act.wait_ge(ss_ready, H * c + h - 1)
                    act.activation(dmat[:, h % 2 * 2:h % 2 * 2 + 2, :],
                                   ps[:, X + h, 0:DV].rearrange("p (a b) -> p a b", a=2), ACT.Square,
                                   accum_out=sumsq[:, h:h + 1]).then_inc(ss_ready, 1)
                act.wait_ge(f_ready, c + 1)
                for h in range(H):
                    act.activation(qk[:, c, h * DV:(h + 1) * DV], ps[:, X + h, 0:DV], ACT.Copy,
                                   scale=factor[:, h:h + 1]).then_inc(hs_ready, 1)
                if c:
                    evac_o(0, c - 1)
                else:
                    splits(20, 21)
            evac_o(0, T - 1)
            splits(22, 23)

            def make_u(event, t, mul, add):
                cut = slice(t * P, (t + 1) * P)
                act.wait_ge(tr_done, 2 * (event + t) + 1)
                for k in range(4):
                    last = act.activation(u_whole[:, k, cut], ps[:, X + 2 * (t % 2), k * P:(k + 1) * P],
                                          ACT.Identity, scale=mul[:, k:k + 1],
                                          bias=0.0 if add is None else add[:, k:k + 1])
                last.then_inc(tr_taken[0], 1)
                for j in range(2):
                    act.wait_ge(tr_taken[j], event + t + 1)
                    act.activation(uhi[:, 4 * j:4 * j + 4, cut], u_whole[:, 4 * j:4 * j + 4, cut],
                                   ACT.Copy).then_inc(ut_hi, 1)

            def make_gate_row(g):
                for half in range(2):
                    act.wait_ge(group_done, g + half + 1)
                    act.activation(gate_row[:, half * HALF:(half + 1) * HALF], ps[:, (g + half) % RING, :],
                                   ACT.Identity, bias=ones[:, 0:1]).then_inc(act_evac, 1)

            def make_xhat(ln, t):
                act.wait_ge(ln_ready, T * ln + t + 1)
                act.activation(resid[:, t, 0:D], resid[:, t, 0:D], ACT.Identity,
                               scale=rstd[:, t % 2, :], bias=nmr[:, t % 2, :]).then_inc(xhat_ready, 1)

            act.wait_ge(gated, T)
            for t in range(T):
                if t == T - 2:
                    splits(26, 27)
                evac_o(1, t)
                if t == 1:
                    make_gate_row(FIRST["gm0"])
                if t == 4:
                    splits(24, 25)
                if t >= 1:
                    make_u(TR_HS, t - 1, fcols[:, 6, :], None)
            splits(28, 29)
            make_u(TR_HS, T - 1, fcols[:, 6, :], None)
            splits(30, 31)

            for t in range(T):
                make_xhat(0, t)
                if t == 3:
                    make_gate_row(FIRST["gf0"])
                if t == 4:
                    splits(32, 33)
                if t >= LAG:
                    make_u(TR_LN0, t - LAG, mulv[:, 1, :], addv[:, 1, :])
            for t in range(T - LAG, T):
                make_u(TR_LN0, t, mulv[:, 1, :], addv[:, 1, :])

            def mlp_up(first, w0, load0, h0, i=0, per=0):
                for u in range(8):
                    f, half = UP[u]
                    cut = slice(half * HALF, (half + 1) * HALF)
                    act.wait_ge(group_done, first + u + 1 + 24 * i)
                    act.activation(h_whole[:, f, cut], ps[:, (first + u) % RING, :], ACT.Relu).then_inc(act_evac, 1)
                    act.wait_ge(relu_sq, h0 + u + 1 + 8 * i)
                    act.activation(hhi[:, f, cut], h_whole[:, f, cut], ACT.Copy).then_inc(h_hi, 1)
                    if w0 + CHUNK_LOADS[u] < N_W:
                        split(load0 + u, w0 + CHUNK_LOADS[u], i, per)

            end = CHUNKS - 1
            with act.Fori(0, end) as i:
                mlp_up(FIRST["mlp0"], W_MLP0, LOADS_MLP0, 0, i, 16)
            act.wait_ge(angle_ready, 1)
            act.activation(rope[:, :, ROT + RH:2 * ROT], angle[:], ACT.Sin)
            act.activation(rope[:, :, 0:RH], turns[:], ACT.Sin).then_inc(sin_ready, 1)
            mlp_up(FIRST["mlp0"] + 24 * end, W_MLP0 + 8 * end, LOADS_MLP0 + 16 * end, 8 * end)
            act.wait_ge(h_ready, 8 * CHUNKS)
            for t in range(T):
                make_xhat(1, t)
                if t >= LAG:
                    make_u(TR_KV, t - LAG, mulv[:, 2, :], addv[:, 2, :])
            splits(98, 99)
            for t in range(T - LAG, T):
                make_u(TR_KV, t, mulv[:, 2, :], addv[:, 2, :])
            splits(100, 101)

            def evac_kt(t):
                act.wait_ge(kt_done, t + 1)
                act.activation(kt[:, :, t * P:(t + 1) * P],
                               ps[:, M, 0:2 * P].rearrange("p (m n) -> p m n", m=2), ACT.Copy).then_inc(kt_evac, 1)

            for t in range(T):
                if t == 3:
                    make_gate_row(FIRST["gm1"])
                if t >= 1:
                    if t == T - 2:
                        splits(102, 103)
                    evac_kt(t - 1)
                    make_u(TR_Q, t - 1, mulv[:, 3, :], addv[:, 3, :])
            evac_kt(T - 1)
            make_u(TR_Q, T - 1, mulv[:, 3, :], addv[:, 3, :])
            splits(104, 105, 106, 107, 108, 109)

            def take_q(pair):
                m = pair % 2
                act.wait_ge(side_t, SIDE.index(("q", pair)) + 1)
                if pair >= 2:
                    act.wait_ge(scores, 2 * pair - 2)
                act.activation(acc[:, m * HALF:(m + 1) * HALF], ps[:, X + 3, :], ACT.Copy,
                               scale=1.0 / math.sqrt(HD)).then_inc(q_taken, 1)

            def exps(n):
                lo, small = P if n < 4 else 0, att[:, n % 3]
                act.wait_ge(max_ready, n + 1)
                for g in range(GROUP):
                    act.activation(probs[:, n % 3, g, lo:], probs[:, n % 3, g, lo:], ACT.Exp,
                                   bias=small[:, 1, g:g + 1], accum_out=small[:, 2, g:g + 1])
                act.activation(small[:, 4, :], small[:, 3, :], ACT.Exp).then_inc(exp_ready, 1)

            def take_pt(n):
                act.wait_ge(p_t, n + 1)
                if n >= 2:
                    act.wait_ge(pv_done, n - 1)
                for j in range(1 if n < 4 else 0, 2):
                    last = act.activation(probst[:, n % 2, j, :], ps[:, X + j, :], ACT.Copy)
                last.then_inc(p_taken, 1)

            def out_hi(pair):
                b, m = pair // 2, pair % 2
                act.wait_ge(side_t, SIDE.index(("o", pair)) + 1)
                act.activation(uhi[:, 4 * m:4 * m + 4, b * P:(b + 1) * P],
                               ps[:, X + 3, :].rearrange("p (k n) -> p k n", k=4), ACT.Copy).then_inc(at_hi, 1)

            def side(n):
                if n % 2 == 1 and (n + 3) // 2 < UNITS // 2:
                    take_q((n + 3) // 2)
                if n % 2 == 0 and n >= 4:
                    out_hi((n - 4) // 2)

            take_q(0)
            take_q(1)
            exps(0)
            for n in range(UNITS):
                if n + 1 < UNITS:
                    exps(n + 1)
                take_pt(n)
                if n < 4:
                    splits((110, 111, 114, 115)[n])
                side(n)
            side(UNITS)
            out_hi(UNITS // 2 - 1)
            splits(112, 113)

            for t in range(T):
                make_xhat(2, t)
                if t == 3:
                    make_gate_row(FIRST["gf1"])
                if t == 4:
                    splits(116, 117)
                if t >= LAG:
                    make_u(TR_LN2, t - LAG, mulv[:, 4, :], addv[:, 4, :])
            for t in range(T - LAG, T):
                make_u(TR_LN2, t, mulv[:, 4, :], addv[:, 4, :])
            with act.Fori(0, end) as i:
                mlp_up(FIRST["mlp1"], W_MLP1, LOADS_MLP1, 8 * CHUNKS, i, 8)
            mlp_up(FIRST["mlp1"] + 24 * end, W_MLP1 + 8 * end, LOADS_MLP1 + 8 * end, 8 * CHUNKS + 8 * end)
            for t in range(T):
                make_xhat(3, t)

        @block.vector
        def _(v):
            step = Steps(v, dve_step)
            v.memset(ones[:], 1.0).then_inc(gate_v, 1)
            v.wait_ge(gate_e, 1)
            v.wait_ge(c_in, 16)
            step.mark(v.tensor_scalar(cs[:, 1, :], cs[:, 1, :], 1.0, None, ALU.add))
            step.mark(v.reciprocal(cs[:, 1, :], cs[:, 1, :]))
            step.mark(v.tensor_tensor(cs[:, 0, :], cs[:, 0, :], cs[:, 1, :], ALU.mult))

            def ada(n, k, i=0, per=0):
                loaded(v, n, i, per)
                if k == 0:
                    ins = v.tensor_scalar(acc[:], stage[:, n % 2, :], cs[:, 0, 0:1], None, ALU.mult)
                else:
                    v.wait_ge(loads_used, n + per * i)
                    ins = v.scalar_tensor_tensor(acc[:], stage[:, n % 2, :], cs[:, 0, k:k + 1], acc[:],
                                                 ALU.mult, ALU.add)
                ins.then_inc(loads_used, 1)

            def adas(vec, ks=range(K)):
                for k in ks:
                    if k == 0 and vec:
                        v.wait_ge(sum_done, vec)
                    ada(NUMBER["ada", vec, k], k)

            def take_mod(vec, i=0):
                v.wait_ge(sum_done, vec + 1 + i)
                dst = mods[:, vec + i, :]
                v.tensor_tensor(dst, ps[:, M, 0:K], dst, ALU.add).then_inc(sum_read, 1)

            def scale(n, w, i=0, per=0):
                if is_scaled(w):
                    loaded(v, n, i, per)
                    src = stage[:, n % 2, :]
                    gate = gate_row[:, 0:D]
                    if W_OUT <= w < W_MLP0 or W_OP <= w < W_MLP1:
                        nh = (w - W_OUT if w < W_MLP0 else w - W_OP) // 4
                        src = src.rearrange("p (k n) -> p k n", k=2)
                        gate = gate[:, nh * HALF:(nh + 1) * HALF].unsqueeze(1).to_broadcast([P, 2, HALF])
                    v.tensor_tensor(src, src, gate, ALU.mult).then_inc(scaled, 1)

            def low(n, w, i=0, per=0):
                v.wait_ge(hi_ready, WEIGHTS_BEFORE[n] + 1 + 8 * i)
                v.tensor_tensor(wlo[:, slot_of(w), :], stage[:, n % 2, :], fr(whi[:, slot_of(w), :]),
                                ALU.subtract).then_inc(loads_used, 1)

            def preps(*blocks):
                for w in blocks:
                    scale(NUMBER["w", w], w)
                    low(NUMBER["w", w], w)

            def modulation(j, sc, sh, ln=None, inv=1.0):
                v.wait_ge(sum_read, max(sc, sh) + 1)
                step.mark(v.tensor_scalar(mulv[:, j, :], mods[:, sc, :], 1.0, inv, ALU.add, ALU.mult))
                if ln is None:
                    step.mark(v.tensor_copy(addv[:, j, :], mods[:, sh, :]))
                    return
                step.mark(v.tensor_tensor(addv[:, j, :], mulv[:, j, :], fcols[:, 3 + ln, :], ALU.mult))
                step.mark(v.tensor_tensor(addv[:, j, :], addv[:, j, :], mods[:, sh, :], ALU.add))
                step.mark(v.tensor_tensor(mulv[:, j, :], mulv[:, j, :], fcols[:, ln, :], ALU.mult))

            def first_u(half):
                cut = slice(half * HALF, (half + 1) * HALF)
                for k in range(K + 2):
                    if k < K:
                        v.tensor_scalar(resid[:, k, cut], resid[:, k, cut], mulv[:, 0, k:k + 1],
                                        addv[:, 0, k:k + 1], ALU.mult, ALU.add).then_inc(u_made, 1)
                    if half == 0 and k == 1:
                        preps(0)
                    if k < 2:
                        continue
                    k -= 2
                    v.wait_ge(u_hi, K * half + k + 1)
                    v.tensor_tensor(ulo[:, k, cut], resid[:, k, cut], fr(uhi[:, k, cut]),
                                    ALU.subtract).then_inc(u_ready, 1)

            for vec, total in ((SC_M0, acc[:]), (SH_M0, gate_row[:, 0:D])):
                for k in range(K):
                    g, part = 2 * vec + k // 4, slice(k % 4 * D, (k % 4 + 1) * D)
                    if k % 4 == 0:
                        v.wait_ge(early_in[g], 16)
                    if k == 0:
                        ins = v.tensor_scalar(total, early_blocks(g)[:, part], cs[:, 0, 0:1], None, ALU.mult)
                    else:
                        v.wait_ge(early_sum, K * vec + k)
                        ins = v.scalar_tensor_tensor(total, early_blocks(g)[:, part], cs[:, 0, k:k + 1], total,
                                                     ALU.mult, ALU.add)
                    ins.then_inc(early_sum, 1)
            v.wait_ge(gate_e, 2)
            v.tensor_tensor(gws[:, :, 8:16], gw[:], fr(gws[:, :, 0:8]), ALU.subtract).then_inc(gate_v, 1)
            v.wait_ge(consts_in, 96)
            take_mod(SC_M0)
            take_mod(SH_M0)
            modulation(0, SC_M0, SH_M0)
            v.wait_ge(xt_in, 16 * K)
            first_u(0)
            first_u(1)
            preps(1, 2, 3, 4, 5, 6)

            v.wait_ge(gate_m, 2)
            v.tensor_tensor(gt[:, 1, :].rearrange("p (g t) -> p g t", t=T),
                            ps[:, M, 0:T * 8].rearrange("p (t g) -> p g t", g=8),
                            gt[:, 0, :].rearrange("p (g t) -> p g t", t=T), ALU.add).then_inc(gate_v, 1)
            v.wait_ge(gate_e, 4)
            v.tensor_scalar(gt[:, 1, :], gt[:, 2, :], CAP, None, ALU.mult).then_inc(gate_v, 1)
            v.wait_ge(gate_e, 5)
            e, e1, rest, log = gt[:, 2, 0:HC], gt[:, 2, HC:2 * HC], gt[:, 3, HC:2 * HC], gt[:, 3, 0:HC]
            v.tensor_scalar(e1, e, 1.0, None, ALU.add).then_inc(gate_v, 1)
            v.wait_ge(gate_v, 5)
            step.mark(v.tensor_scalar(rest, e1, -1.0, None, ALU.add))
            step.mark(v.tensor_tensor(rest, e, rest, ALU.subtract))
            v.wait_ge(gate_e, 6)
            step.mark(v.reciprocal(e1, e1))
            step.mark(v.tensor_tensor(rest, rest, e1, ALU.mult))
            step.mark(v.tensor_tensor(log, log, rest, ALU.add))
            v.tensor_scalar(gt[:, 1, HC:2 * HC], log, -1.0, None, ALU.mult).then_inc(gate_v, 1)
            preps(7)
            row = scratch[0:HC].rearrange("p a (b n) -> p (a b) n", n=P)
            v.memset(row[:, 7, :], 0.0)
            v.wait_ge(gate_m, 3)
            step.mark(v.tensor_copy(row[:, 0:2, :], ps[0:HC, M, 0:2 * P].rearrange("p (a n) -> p a n", a=2)))
            step.mark(v.tensor_tensor_scan(row[:, 2, :], row[:, 1, :], row[:, 7, :], 0.0, ALU.add, ALU.add))
            step.mark(v.tensor_tensor(row[:, 3, :], row[:, 0, :], row[:, 2, :], ALU.subtract))
            v.tensor_tensor_scan(row[:, 4, :], row[:, 3, :], row[:, 3, :], MASKED, ALU.max,
                                 ALU.max).then_inc(gate_v, 1)
            preps(8)
            adas(G_M0, range(2))
            ends, sums = gt[0:1, 3, 0:HC], gt[0:1, 3, HC:2 * HC]
            m_row, m_prev = gt[0:1, 2, 0:HC], gt[0:1, 2, HC:2 * HC]
            v.wait_ge(gate_m, 4)
            step.mark(v.tensor_copy(gt[0:1, 3, :], ps[0:1, M, 0:2 * HC]))
            step.mark(v.tensor_tensor(sums, ends, sums, ALU.add))
            for h in range(H):
                part = slice(h * T, (h + 1) * T)
                step.mark(v.tensor_tensor_scan(m_row[:, part], ends[:, part], sums[:, part], 0.0,
                                               ALU.add, ALU.max))
            step.mark(v.memset(m_prev, 0.0))
            v.tensor_copy(m_prev.rearrange("p (h t) -> p h t", t=T)[:, :, 1:T],
                          m_row.rearrange("p (h t) -> p h t", t=T)[:, :, 0:T - 1]).then_inc(gate_v, 1)
            preps(9)
            adas(G_M0, range(2, 4))
            v.wait_ge(gate_m, 5)
            step.mark(v.tensor_copy(m_prev_col, ps[0:HC, M, 0:1]))
            step.mark(v.tensor_scalar(row[:, 4, :], row[:, 4, :], m_prev_col, None, ALU.max))
            v.tensor_scalar(negm[:], row[:, 4, :], -1.0, None, ALU.mult).then_inc(gate_v, 1)
            v.tensor_tensor(row[:, 7, :], row[:, 2, :], row[:, 4, :], ALU.add).then_inc(gate_v, 1)
            preps(10)
            adas(G_M0, range(4, K))
            v.memset(cstate[:], 0.0)
            v.wait_ge(gate_m, 6)
            v.tensor_copy(cols[:], ps[:, M, 0:5 * HC].rearrange("p (a n) -> p a n", a=5)).then_inc(gate_v, 1)
            v.memset(resid[:].rearrange("p t (h n) -> p t h n", h=H)[:, :, :, DV:DV + 1], 1.0)
            preps(11, 12, 13)
            take_mod(G_M0)

            def evac_v(nh, t):
                g = FIRST["v"] + T * nh + t
                v.wait_ge(group_done, g + 1)
                dst = resid[:, t, :].rearrange("p (h n) -> p h n", h=H)[:, 2 * nh:2 * nh + 2, 0:DV]
                v.tensor_copy(dst, ps[:, g % RING, :].rearrange("p (h n) -> p h n", h=2)).then_inc(dve_evac, 1)

            for t in range(T):
                adas(SH_F0, range(t, t + 1))
                if t == T - 1:
                    preps(14, 15)
                evac_v(0, t)
            for t in range(T):
                evac_v(1, t)
                adas(SC_F0, range(t, t + 1))
                if t == 0:
                    take_mod(SH_F0)
                if t in (1, 2):
                    preps(15 + t)
            preps(18, 19)

            def apply_gate(nh, t):
                e = gate_tanh(nh, t)
                v.wait_ge(act_evac, ACT_BEFORE[o_group(nh, t)] + 1)
                v.wait_ge(hs_ready, H * (t + 1))
                part = qk[:, t, nh * HALF:(nh + 1) * HALF]
                v.scalar_tensor_tensor(part, e, 1.0, part, ALU.add, ALU.mult).then_inc(gated, 1)

            for c in range(T):
                v.wait_ge(mix, 4 * c + 4)
                v.tensor_tensor(qk[:, c, 0:H * P], ps[:, X + 3, :], qk[:, c, 0:H * P], ALU.mult).then_inc(s_ready, 1)
                v.wait_ge(d_masked, c + 1)
                v.tensor_tensor(smat[:].rearrange("p h n -> p (h n)"), ps[:, X + 1, :],
                                dmat[:].rearrange("p h n -> p (h n)"), ALU.mult).then_inc(s_ready, 1)
                if c == 0:
                    take_mod(SC_F0)
                if c == 4:
                    take_mod(G_F0)
                adas((G_F0, SH_KV)[c // 4], range(2 * (c % 4), 2 * (c % 4) + 2))
                r = stats[:, 0, 0:H]
                v.wait_ge(ss_ready, H * (c + 1))
                step.mark(v.tensor_copy(r, ps[:, X:X + H, DV]))
                step.mark(v.scalar_tensor_tensor(r, r, -1.0, r, ALU.mult, ALU.max))
                step.mark(v.tensor_tensor(r, r, cols[:, 3, :].rearrange("p (h t) -> p h t", t=T)[:, :, c],
                                          ALU.max))
                step.mark(v.reciprocal(r, r))
                step.mark(v.tensor_tensor(mean, sumsq, r, ALU.mult))
                step.mark(v.tensor_tensor(mean, mean, r, ALU.mult))
                v.tensor_scalar(mean, mean, 1.0 / DV, RMS_EPS, ALU.mult, ALU.add).then_inc(ms_ready, 1)
                v.wait_ge(rms_ready, c + 1)
                v.tensor_tensor(factor, mean, r, ALU.mult).then_inc(f_ready, 1)
                if c:
                    apply_gate(0, c - 1)
                else:
                    preps(20, 21)
                if c < T - 1:
                    for h in range(H):
                        v.wait_ge(state_done, H * c + h + 1)
                        v.scalar_tensor_tensor(cstate[:, h, :], cstate[:, h, :],
                                               cols[:, 4, h * T + c:h * T + c + 1],
                                               ps[:, X + h, 0:DV + 1], ALU.mult, ALU.add).then_inc(c_updated, 1)
            take_mod(SH_KV)
            apply_gate(0, T - 1)
            step.mark(v.tensor_scalar(fcols[:, 6, :], fcols[:, 6, :], 0.5, None, ALU.mult))
            preps(22, 23)

            def diagonal(vec):
                v.wait_ge(sum_read, vec + 1)
                for k in range(K):
                    last = v.tensor_scalar(acc[:, k * P:(k + 1) * P], ident[:], mods[:, vec, k:k + 1], None,
                                           ALU.mult)
                last.then_inc(diag_ready, 1)

            def gate_row_made(name):
                v.wait_ge(act_evac, ACT_BEFORE[FIRST[name] + 2])

            def take_u(event, t, mul, add):
                cut = slice(t * P, (t + 1) * P)
                v.wait_ge(tr_done, 2 * (event + t) + 2)
                for k in range(4):
                    src = ps[:, X + 2 * (t % 2) + 1, k * P:(k + 1) * P]
                    if add is None:
                        last = v.tensor_scalar(u_whole[:, 4 + k, cut], src, mul[:, 4 + k:5 + k], None, ALU.mult)
                    else:
                        last = v.tensor_scalar(u_whole[:, 4 + k, cut], src, mul[:, 4 + k:5 + k],
                                               add[:, 4 + k:5 + k], ALU.mult, ALU.add)
                last.then_inc(tr_taken[1], 1)

            def make_lo(event, t):
                for j in range(2):
                    v.wait_ge(ut_hi, 2 * (event + t) + j + 1)
                    cut = slice(t * P, (t + 1) * P)
                    v.tensor_tensor(ulo[:, 4 * j:4 * j + 4, cut], u_whole[:, 4 * j:4 * j + 4, cut],
                                    fr(uhi[:, 4 * j:4 * j + 4, cut]), ALU.subtract).then_inc(ut_ready, 1)

            diagonal(G_M0)
            for t in range(T):
                if t == 4:
                    gate_row_made("gm0")
                    preps(24, 25)
                if t == T - 2:
                    preps(26, 27)
                apply_gate(1, t)
                if t >= 1:
                    take_u(TR_HS, t - 1, fcols[:, 6, :], None)
                if t >= 2:
                    make_lo(TR_HS, t - 2)
            make_lo(TR_HS, T - 2)
            preps(28, 29)
            take_u(TR_HS, T - 1, fcols[:, 6, :], None)
            make_lo(TR_HS, T - 1)

            def norm(ln, t):
                j = t % 2
                if t >= LAG:
                    v.wait_ge(xhat_ready, T * ln + t - 1)
                for half in range(2):
                    step.mark(v.bn_stats(stats[:, j, 6 * half:6 * half + 6],
                                         resid[:, t, half * HALF:(half + 1) * HALF]))
                v.bn_aggr(moments[:, j, :], stats[:, j, :]).then_inc(moments_ready, 1)

            def add_out(g, t, nh, alpha):
                v.wait_ge(group_done, g + 1)
                dst = resid[:, t, nh * HALF:(nh + 1) * HALF]
                v.scalar_tensor_tensor(dst, dst, alpha, ps[:, g % RING, :], ALU.mult,
                                       ALU.add).then_inc(dve_evac, 1)

            v.wait_ge(x_in, 16 * T)
            for t in range(T):
                if t == T - 1:
                    preps(30, 31)
                add_out(FIRST["out0"] + t, t, 0, ALPHA)
            modulation(1, SC_F0, SH_F0, ln=0)
            diagonal(G_F0)
            for t in range(T):
                g = half_group("out1", t)
                add_out(g, t, 1, ALPHA)
                v.wait_ge(dve_evac, DVE_BEFORE[g] + 1)
                norm(0, t)
                if t == 4:
                    gate_row_made("gf0")
                    preps(32, 33)
                if t >= LAG:
                    take_u(TR_LN0, t - LAG, mulv[:, 1, :], addv[:, 1, :])
                if t > LAG:
                    make_lo(TR_LN0, t - LAG - 1)
            make_lo(TR_LN0, T - LAG - 1)
            for t in range(T - LAG, T):
                take_u(TR_LN0, t, mulv[:, 1, :], addv[:, 1, :])
                make_lo(TR_LN0, t)

            def angles():
                v.wait_ge(rope_in, 48)
                pos = rope[:, 0, 0:T]
                step.mark(v.tensor_copy(pos, posi[:]))
                step.mark(v.tensor_tensor(angle[:], pos.unsqueeze(2).to_broadcast([P, T, RH]),
                                          turns[:, 0, :].unsqueeze(1).to_broadcast([P, T, RH]), ALU.mult))
                step.mark(v.tensor_scalar(turns[:], angle[:], 1.0 / (2 * math.pi), ROUNDER, ALU.mult, ALU.add))
                step.mark(v.tensor_scalar(turns[:], turns[:], -ROUNDER, None, ALU.add))
                for part in TWO_PI:
                    step.mark(v.scalar_tensor_tensor(angle[:], turns[:], -part, angle[:], ALU.mult, ALU.add))
                step.mark(v.tensor_scalar(angle[:], angle[:], PI_IN, -PI_IN, ALU.min, ALU.max))
                step.mark(v.tensor_scalar(turns[:], angle[:], math.pi / 2, None, ALU.add))
                wrap = rope[:, :, 0:RH]
                step.mark(v.tensor_scalar(wrap, turns[:], math.pi, -2 * math.pi, ALU.is_gt, ALU.mult))
                step.mark(v.tensor_tensor(turns[:], turns[:], wrap, ALU.add))
                v.tensor_scalar(turns[:], turns[:], PI_IN, -PI_IN, ALU.min, ALU.max).then_inc(angle_ready, 1)

            def mlp_chunk(first, w0, load0, h0, i=0, per=0, with_ada=False, tail=None):
                for u in range(8):
                    f, half = UP[u]
                    cut = slice(half * HALF, (half + 1) * HALF)
                    q = h_whole[:, f, cut]
                    w = w0 + CHUNK_LOADS[u]
                    v.wait_ge(act_evac, ACT_BEFORE[first + u] + 1 + 8 * i)
                    v.tensor_tensor(q, q, q, ALU.mult).then_inc(relu_sq, 1)
                    if w < N_W:
                        scale(load0 + u, w, i, per)
                    v.wait_ge(h_hi, h0 + u + 1 + 8 * i)
                    v.tensor_tensor(hlo[:, f, cut], q, fr(hhi[:, f, cut]), ALU.subtract).then_inc(h_ready, 1)
                    if w < N_W:
                        low(load0 + u, w, i, per)
                v.wait_ge(h_written, T if w0 < W_KV else 3 * T)
                for d in range(16):
                    t, nh = d // 2, d % 2
                    g = first + 8 + d
                    v.wait_ge(group_done, g + 1 + 24 * i)
                    v.wait_ge(dve_evac, DVE_BEFORE[g] - 15 + 16 * i)
                    dst = resid[:, t, nh * HALF:(nh + 1) * HALF]
                    v.tensor_tensor(dst, ps[:, g % RING, :], dst, ALU.add).then_inc(dve_evac, 1)
                    if with_ada and 1 <= d <= K:
                        if d == 1:
                            v.wait_ge(sum_done, SC_KV + i)
                        ada(load0 + 8 + d - 1, d - 1, i, per)
                    if with_ada and d == 14:
                        take_mod(SC_KV, i)
                    if tail and nh == 1:
                        v.wait_ge(dve_evac, DVE_BEFORE[g] + 1)
                        tail(t)

            end = CHUNKS - 1
            with v.Fori(0, end) as i:
                mlp_chunk(FIRST["mlp0"], W_MLP0, LOADS_MLP0, 0, i, 16, with_ada=True)
            angles()
            modulation(2, SC_KV, SH_KV, ln=1)
            modulation(3, SC_M1, SH_M1, inv=1.0 / ALPHA)
            modulation(4, SC_F1, SH_F1, ln=2)

            def tail_kv(t):
                norm(1, t)
                if t >= LAG:
                    take_u(TR_KV, t - LAG, mulv[:, 2, :], addv[:, 2, :])
                if t > LAG:
                    make_lo(TR_KV, t - LAG - 1)

            mlp_chunk(FIRST["mlp0"] + 24 * end, W_MLP0 + 8 * end, LOADS_MLP0 + 16 * end, 8 * end, tail=tail_kv)
            make_lo(TR_KV, T - LAG - 1)
            preps(98, 99)
            for t in range(T - LAG, T):
                take_u(TR_KV, t, mulv[:, 2, :], addv[:, 2, :])
                make_lo(TR_KV, t)
            preps(100, 101)

            v.wait_ge(sin_ready, 1)
            v.tensor_copy(rope[:, :, RH:ROT], rope[:, :, 0:RH])
            step.mark(v.tensor_scalar(rope[:, :, ROT:ROT + RH], rope[:, :, ROT + RH:2 * ROT], -1.0, None, ALU.mult))

            def rotate(src, dst, heads, t):
                def table(a, n):
                    return rope[:, t, a:a + n].unsqueeze(1).to_broadcast([P, heads, n])

                part = rtmp[:, :, 0:heads, :]
                step.mark(v.tensor_copy(dst, src))
                v.tensor_tensor(part[:, 1, :, 0:RH], src[:, :, RH:ROT], table(ROT, RH), ALU.mult)
                step.mark(v.tensor_tensor(part[:, 1, :, RH:ROT], src[:, :, 0:RH], table(ROT + RH, RH), ALU.mult))
                ins = v.tensor_tensor(part[:, 0], src[:, :, 0:ROT], table(0, ROT), ALU.mult)
                ins.then_inc(dve_evac, 1)

            def finish_rotation(dst, heads):
                part = rtmp[:, :, 0:heads, :]
                v.tensor_tensor(dst[:, :, 0:ROT], part[:, 0], part[:, 1], ALU.add).then_inc(roped, 1)

            for t in range(T):
                g = kv_group(t)
                if t == 1:
                    diagonal(G_M1)
                if t == T - 2:
                    preps(102, 103)
                v.wait_ge(group_done, g + 1)
                src = ps[:, g % RING, :].rearrange("p (h d) -> p h d", d=HD)
                if t >= 2:
                    v.wait_ge(kt_done, t - 1)
                dst = probs[:, t % 2, 0, :].rearrange("p (h d) -> p h d", d=HD)
                step.mark(v.tensor_copy(vv[:, t, :], ps[:, g % RING, 4 * HD:8 * HD]))
                rotate(src[:, 0:4], dst, 4, t)
                v.wait_ge(dve_evac, DVE_BEFORE[g] + 1)
                finish_rotation(dst, 4)
                if t >= 1:
                    take_u(TR_Q, t - 1, mulv[:, 3, :], addv[:, 3, :])
                if t >= 2:
                    make_lo(TR_Q, t - 2)
            take_u(TR_Q, T - 1, mulv[:, 3, :], addv[:, 3, :])
            make_lo(TR_Q, T - 2)
            make_lo(TR_Q, T - 1)
            gate_row_made("gm1")
            preps(104, 105)
            v.wait_ge(spilled, 16 * T)
            for nh in range(2):
                for t in range(T):
                    g = FIRST["q"] + T * nh + t
                    if t == T - 1 and nh == 0:
                        preps(106, 107)
                    v.wait_ge(group_done, g + 1)
                    v.wait_ge(roped, T + T * nh + t)
                    dst = resid[:, t, nh * HALF:(nh + 1) * HALF].rearrange("p (h d) -> p h d", d=HD)
                    rotate(ps[:, g % RING, :].rearrange("p (h d) -> p h d", d=HD), dst, 8, t)
                    v.wait_ge(dve_evac, DVE_BEFORE[g] + 1)
                    finish_rotation(dst, 8)
                if nh == 0:
                    preps(108, 109)

            def maxima(n):
                lo, u = (P if n < 4 else 0), n % 4
                small = att[:, n % 3]
                v.wait_ge(scores, n + 1)
                if n >= 3:
                    v.wait_ge(p_t, n - 2)
                for g in range(GROUP):
                    bank, at = 2 * (n % 2) + g // 2, g % 2 * 2 * P
                    last = v.tensor_tensor_reduce(probs[:, n % 3, g, lo:], ps[:, bank, at + lo:at + 2 * P],
                                                  mask[:, lo:], 1.0, sinks[:, 4 * u + g:4 * u + g + 1],
                                                  ALU.add, ALU.max, small[:, 0, g:g + 1])
                step.mark(last)
                step.mark(v.tensor_scalar(small[:, 1, :], small[:, 0, :], -1.0, None, ALU.mult))
                v.tensor_tensor(small[:, 3, :], small[:, 1, :], sinks[:, 4 * u:4 * u + 4],
                                ALU.add).then_inc(max_ready, 1)

            def totals(n):
                small = att[:, n % 3]
                v.wait_ge(exp_ready, n + 1)
                step.mark(v.tensor_tensor(small[:, 5, :], small[:, 2, :], small[:, 4, :], ALU.add))
                step.mark(v.reciprocal(small[:, 5, :], small[:, 5, :]))

            def take_out(n):
                b, u = n // 4, n % 4
                v.wait_ge(pv_done, n + 1)
                dst = resid[:, b, u * GROUP * HD:(u + 1) * GROUP * HD].rearrange("p (g d) -> p g d", g=GROUP)
                v.tensor_tensor(dst, ps[:, X + 2, 0:GROUP * HD].rearrange("p (g d) -> p g d", g=GROUP),
                                att[:, n % 3, 5, :].unsqueeze(2).to_broadcast([P, GROUP, HD]),
                                ALU.mult).then_inc(out_ready, 1)

            def out_lo(pair):
                b, m = pair // 2, pair % 2
                cut = slice(b * P, (b + 1) * P)
                v.wait_ge(at_hi, pair + 1)
                v.tensor_tensor(ulo[:, 4 * m:4 * m + 4, cut], ps[:, X + 3, :].rearrange("p (k n) -> p k n", k=4),
                                fr(uhi[:, 4 * m:4 * m + 4, cut]), ALU.subtract).then_inc(at_ready, 1)

            v.wait_ge(att_in, 16)
            maxima(0)
            maxima(1)
            for n in range(UNITS + 1):
                if n + 2 < UNITS:
                    maxima(n + 2)
                if n < UNITS:
                    totals(n)
                if n < 4:
                    preps((110, 111, 114, 115)[n])
                if n % 2 == 0 and n >= 4:
                    out_lo((n - 4) // 2)
                if n:
                    take_out(n - 1)
            out_lo(UNITS // 2 - 1)
            v.wait_ge(resid_in, 16 * T)
            for t in range(T):
                if t == T - 1:
                    preps(112, 113)
                add_out(FIRST["op0"] + t, t, 0, 1.0)
            diagonal(G_F1)
            for t in range(T):
                g = half_group("op1", t)
                add_out(g, t, 1, 1.0)
                v.wait_ge(dve_evac, DVE_BEFORE[g] + 1)
                norm(2, t)
                if t == 4:
                    gate_row_made("gf1")
                    preps(116, 117)
                if t >= LAG:
                    take_u(TR_LN2, t - LAG, mulv[:, 4, :], addv[:, 4, :])
                if t > LAG:
                    make_lo(TR_LN2, t - LAG - 1)
            make_lo(TR_LN2, T - LAG - 1)
            for t in range(T - LAG, T):
                take_u(TR_LN2, t, mulv[:, 4, :], addv[:, 4, :])
                make_lo(TR_LN2, t)
            with v.Fori(0, end) as i:
                mlp_chunk(FIRST["mlp1"], W_MLP1, LOADS_MLP1, 8 * CHUNKS, i, 8)

            def final(t):
                v.wait_ge(xhat_ready, 3 * T + t + 1)
                tile = resid[:, t, 0:D]
                step.mark(v.tensor_tensor(tile, tile, lnrows[:, 0, :], ALU.mult))
                v.tensor_tensor(tile, tile, lnrows[:, 1, :], ALU.add).then_inc(final_ready, 1)

            def tail_out(t):
                norm(3, t)
                if t >= 1:
                    final(t - 1)

            v.wait_ge(rows_in, 128)
            mlp_chunk(FIRST["mlp1"] + 24 * end, W_MLP1 + 8 * end, LOADS_MLP1 + 8 * end, 8 * CHUNKS + 8 * end,
                      tail=tail_out)
            final(T - 1)

        @block.tensor
        def _(pe):
            def product(dst, left_hi, left_lo, right_hi, right_lo, start, stop):
                pe.matmul(dst, left_hi, right_hi, start=start, stop=False)
                pe.matmul(dst, left_hi, right_lo, start=False, stop=False)
                return pe.matmul(dst, left_lo, right_hi, start=False, stop=stop)

            def need(w):
                pe.wait_ge(loads_used, NUMBER["w", w] + 1)

            def sum_vector(vec, i=0, load=None, per=0):
                total = gate_row if vec == SH_M0 else acc
                if vec <= SH_M0:
                    pe.wait_ge(early_sum, K * (vec + 1))
                else:
                    pe.wait_ge(loads_used, (NUMBER["ada", vec, K - 1] if load is None else load) + 1 + per * i)
                if vec:
                    pe.wait_ge(sum_read, vec + i)
                for k in range(K):
                    last = pe.matmul(ps[:, M, k:k + 1], total[:, k * P:(k + 1) * P], ones[:, 0:1], start=True,
                                     stop=True)
                last.then_inc(sum_done, 1)

            def build_row(g, n):
                pe.wait_ge(diag_ready, n)
                for half in range(2):
                    wait_evac(pe, g + half)
                    for k in range(4):
                        last = pe.matmul(ps[:, (g + half) % RING, k * P:(k + 1) * P],
                                         ones[:, 0:1].to_broadcast([P, P]),
                                         acc[:, (4 * half + k) * P:(4 * half + k + 1) * P], start=True, stop=True)
                    last.then_inc(group_done, 1)

            def by_token(g, w0, t, part=(0, 1, 2, 3)):
                for j in part:
                    w = w0 + j
                    if t == 0:
                        need(w)
                    if j == 0:
                        wait_evac(pe, g)
                    s = slot_of(w)
                    for kk in range(2):
                        k = 2 * j + kk
                        cut, col = slice(t * P, (t + 1) * P), slice(kk * HALF, (kk + 1) * HALF)
                        last = product(ps[:, g % RING, :], uhi[:, k, cut], ulo[:, k, cut], whi[:, s, col],
                                       wlo[:, s, col], start=(j == 0 and kk == 0), stop=(j == 3 and kk == 1))
                    if t == T - 1 and j < 3:
                        last.then_inc(released, 1)
                if part[-1] == 3:
                    last.then_inc(group_done, 1)

            def last_two(g, w0):
                for n in range(2):
                    wait_evac(pe, g + n)
                for j in range(4):
                    s = slot_of(w0 + j)
                    for n in range(2):
                        cut = slice((T - 2 + n) * P, (T - 1 + n) * P)
                        for kk in range(2):
                            k, col = 2 * j + kk, slice(kk * HALF, (kk + 1) * HALF)
                            last = product(ps[:, (g + n) % RING, :], uhi[:, k, cut], ulo[:, k, cut], whi[:, s, col],
                                           wlo[:, s, col], start=(j == 0 and kk == 0), stop=(j == 3 and kk == 1))
                        if j == 3:
                            last.then_inc(group_done, 1)
                    if j < 3:
                        last.then_inc(released, 1)

            def transpose_tile(event, t, src):
                for j in range(2):
                    n = 2 * (event + t) + j
                    if n >= 4:
                        pe.wait_ge(tr_taken[j], n // 2 - 1)
                    for k in range(4):
                        last = pe.transpose(ps[:, X + n % 4, k * P:(k + 1) * P],
                                            src[:, (4 * j + k) * P:(4 * j + k + 1) * P], ident[:])
                    last.then_inc(tr_done, 1)

            pe.wait_ge(consts_in, 96)
            pe.wait_ge(gate_v, 1)
            sum_vector(SC_M0)
            sum_vector(SH_M0)

            def qk_head(n):
                need(n)
                for half in range(2):
                    g = FIRST["qk"] + 2 * n + half
                    wait_evac(pe, g)
                    cut = slice(half * HALF, (half + 1) * HALF)
                    s = slot_of(n)
                    for k in range(K):
                        if n == 0:
                            pe.wait_ge(u_ready, K * half + k + 1)
                        col = slice(k * P, (k + 1) * P)
                        last = product(ps[:, g % RING, :], whi[:, s, col], wlo[:, s, col], uhi[:, k, cut],
                                       ulo[:, k, cut], start=(k == 0), stop=(k == K - 1))
                    last.then_inc(group_done, 1)

            qk_head(0)
            pe.wait_ge(gate_v, 2)
            for half in range(2):
                cut = slice(half * HALF, (half + 1) * HALF)
                for k in range(K):
                    pe.matmul(ps[0:16, X + half, :], gws[:, k, :], uhi[:, k, cut], start=(k == 0), stop=False)
                    last = pe.matmul(ps[0:16, X + half, :], gws[:, k, :], ulo[:, k, cut], start=False,
                                     stop=(k == K - 1))
            last.then_inc(gate_m, 1)
            qk_head(1)
            pe.wait_ge(gate_e, 3)
            pe.wait_ge(sum_read, 2)
            for t in range(T):
                last = pe.matmul(ps[:, M, t * 8:(t + 1) * 8], scratch[0:16, t // 4, t % 4 * P:(t % 4 + 1) * P],
                                 pair_sum[:], start=True, stop=True)
            last.then_inc(gate_m, 1)
            qk_head(2)
            pe.wait_ge(gate_v, 6)
            for j in range(2):
                last = pe.transpose(ps[0:HC, M, j * P:(j + 1) * P], gt[:, 1, j * HC:(j + 1) * HC], ident[:])
            last.then_inc(gate_m, 1)
            qk_head(3)
            row = scratch[0:HC].rearrange("p a (b n) -> p (a b) n", n=P)
            pe.wait_ge(gate_v, 7)
            for j, r in enumerate((2, 4)):
                last = pe.matmul(ps[0:1, M, j * HC:(j + 1) * HC], row[:, r, P - 1:P], ident[0:HC, 0:HC],
                                 start=True, stop=True)
            last.then_inc(gate_m, 1)
            qk_head(4)
            pe.wait_ge(gate_v, 8)
            pe.matmul(ps[0:HC, M, 0:1], gt[0:1, 2, HC:2 * HC], ones[0:1, 0:1], start=True,
                      stop=True).then_inc(gate_m, 1)
            qk_head(5)
            pe.wait_ge(gate_e, 7)
            for j, src in enumerate((row[:, 3, :], winter[:], row[:, 5, :], row[:, 6, :])):
                pe.transpose(ps[:, M, j * HC:(j + 1) * HC], src, ident[0:HC, 0:HC])
            pe.matmul(ps[:, M, 4 * HC:5 * HC], winter[:, P - 1:P].to_broadcast([HC, P]), ident[0:HC, 0:HC],
                      start=True, stop=True).then_inc(gate_m, 1)
            for n in (6, 7):
                qk_head(n)
            pe.wait_ge(gate_v, 11)
            sum_vector(G_M0)

            for nh in range(2):
                for t in range(T):
                    g = FIRST["v"] + T * nh + t
                    by_token(g, W_V + 4 * nh, t)
                    if nh == 1 and t == 0:
                        sum_vector(SH_F0)

            def chunk_rows(c, dst, src):
                for h in range(H):
                    r = h * T + c
                    last = pe.matmul(ps[:, dst, h * P:(h + 1) * P], ident[0:HC, r:r + 1].to_broadcast([HC, P]),
                                     src[:], start=True, stop=True)
                last.then_inc(mix, 1)

            pe.wait_ge(act_evac, 16)
            pe.wait_ge(dve_evac, 16)
            for c in range(T):
                if c:
                    pe.wait_ge(c_updated, H * (c - 1) + 1)
                chunk_rows(c, X, negm)
                if c:
                    pe.wait_ge(c_updated, H * (c - 1) + 2)
                for h in range(H):
                    last = pe.matmul(ps[:, X + 1, h * P:(h + 1) * P], qk[:, c, (H + h) * P:(H + h + 1) * P],
                                     qk[:, c, h * P:(h + 1) * P], start=True, stop=True)
                last.then_inc(mix, 1)
                if c:
                    pe.wait_ge(c_updated, H * (c - 1) + 3)
                for h in range(H):
                    last = pe.transpose(ps[:, X + 2, h * P:(h + 1) * P], qk[:, c, (H + h) * P:(H + h + 1) * P],
                                        ident[:])
                last.then_inc(mix, 1)
                if c:
                    pe.wait_ge(c_updated, H * c)
                chunk_rows(c, X + 3, winter)
                if c in (0, 4):
                    sum_vector((SC_F0, G_F0)[c // 4])
                if c:
                    by_token(FIRST["o0"] + c - 1, W_O, c - 1, part=(0, 1))
                pe.wait_ge(s_ready, 2 * c + 2)
                pe.wait_ge(ktok_ready, c + 1)
                for h in range(H):
                    val = resid[:, c, h * (DV + 1):(h + 1) * (DV + 1)]
                    pe.matmul(ps[:, X + h, 0:DV + 1], smat[:, h, :], val, start=True, stop=False)
                    pe.matmul(ps[:, X + h, 0:DV + 1], qk[:, c, h * P:(h + 1) * P], cstate[:, h, :], start=False,
                              stop=True).then_inc(num_done, 1)
                if c:
                    by_token(FIRST["o0"] + c - 1, W_O, c - 1, part=(2, 3))
                if c < T - 1:
                    for h in range(H):
                        pe.wait_ge(hs_ready, H * c + h + 1)
                        val = resid[:, c, h * (DV + 1):(h + 1) * (DV + 1)]
                        pe.matmul(ps[:, X + h, 0:DV + 1], ktok[:, h, :], val, start=True,
                                  stop=True).then_inc(state_done, 1)
            sum_vector(SH_KV)
            by_token(FIRST["o0"] + T - 1, W_O, T - 1)
            pe.wait_ge(hs_ready, H * T)
            for t in range(T):
                if t < T - 2:
                    by_token(o_group(1, t), W_O + 4, t)
                elif t == T - 2:
                    last_two(o_group(1, t), W_O + 4)
                if t == 1:
                    build_row(FIRST["gm0"], 1)
                if t >= 1:
                    pe.wait_ge(gated, T + t)
                    transpose_tile(TR_HS, t - 1, qk[:, t - 1, :])
            for t in range(T):
                pe.wait_ge(ut_ready, 2 * (TR_HS + t) + 2)
                by_token(FIRST["out0"] + t, W_OUT, t)
                if t == 0:
                    pe.wait_ge(gated, 2 * T)
                    transpose_tile(TR_HS, T - 1, qk[:, T - 1, :])

            def normed(event, ln, t):
                pe.wait_ge(xhat_ready, T * ln + t + 1)
                transpose_tile(event, t, resid[:, t, :])

            def second_half(name, gate, n, w0, ln, event):
                for t in range(T):
                    g = half_group(name, t)
                    by_token(g, w0, t)
                    if t == 3:
                        build_row(FIRST[gate], n)
                    if t >= LAG:
                        normed(event, ln, t - LAG)

            second_half("out1", "gf0", 2, W_OUT + 4, 0, TR_LN0)

            def mlp_chunk(first, w0, load0, h0, i=0, per=0, with_ada=False, tail=None, head=None):
                for u in range(8):
                    f, half = UP[u]
                    g = first + u
                    if half == 0:
                        pe.wait_ge(loads_used, load0 + (CHUNK_LOADS.index(f) + 1 if f >= 2 else 0) + per * i)
                    pe.wait_ge(ut_ready, 2 * ((TR_LN0 if w0 < W_KV else TR_LN2) + T // 2 * (half + 1)))
                    wait_evac(pe, g, i, 16 if ENGINES[g - RING] == "D" else 8)
                    cut = slice(half * HALF, (half + 1) * HALF)
                    for k in range(K):
                        col = slice(k * P, (k + 1) * P)
                        last = product(ps[:, g % RING, :], whi[:, f % 2, col], wlo[:, f % 2, col],
                                       uhi[:, k, cut], ulo[:, k, cut], start=(k == 0), stop=(k == K - 1))
                    last.then_inc(group_done, 1)
                    if head and u < LAG:
                        head(T - LAG + u)
                pe.wait_ge(loads_used, load0 + CHUNK_LOADS.index(7) + 1 + per * i)
                for d in range(16):
                    t, nh = d // 2, d % 2
                    g = first + 8 + d
                    if d in (0, 8):
                        pe.wait_ge(h_ready, h0 + (6 if d == 0 else 8) + 8 * i)
                    wait_evac(pe, g, i, 16 if ENGINES[g - RING] == "D" else 8)
                    cut, col = slice(t * P, (t + 1) * P), slice(nh * HALF, (nh + 1) * HALF)
                    for f in range(4):
                        last = product(ps[:, g % RING, :], hhi[:, f, cut], hlo[:, f, cut], whi[:, 2 + f, col],
                                       wlo[:, 2 + f, col], start=(f == 0), stop=(f == 3))
                    last.then_inc(group_done, 1)
                    if with_ada and d == 11:
                        sum_vector(SC_KV, i, load0 + 15, per)
                    if tail and nh == 1 and t >= LAG:
                        tail(t - LAG)

            end = CHUNKS - 1
            mlp_chunk(FIRST["mlp0"], W_MLP0, LOADS_MLP0, 0, with_ada=True, head=lambda t: normed(TR_LN0, 0, t))
            with pe.Fori(1, end) as i:
                mlp_chunk(FIRST["mlp0"], W_MLP0, LOADS_MLP0, 0, i, 16, with_ada=True)
            mlp_chunk(FIRST["mlp0"] + 24 * end, W_MLP0 + 8 * end, LOADS_MLP0 + 16 * end, 8 * end,
                      tail=lambda t: normed(TR_KV, 1, t))
            normed(TR_KV, 1, T - 2)

            def k_transposed(t):
                pe.wait_ge(roped, t + 1)
                if t:
                    pe.wait_ge(kt_evac, t)
                else:
                    pe.wait_ge(sum_read, NVEC)
                for m in range(2):
                    last = pe.transpose(ps[:, M, m * P:(m + 1) * P], probs[:, t % 2, 0, m * P:(m + 1) * P], ident[:])
                last.then_inc(kt_done, 1)

            def q_input(t):
                pe.wait_ge(h_written, T + t + 1)
                transpose_tile(TR_Q, t, resid[:, t, :])

            for t in range(T):
                if t < T - 2:
                    pe.wait_ge(ut_ready, 2 * (TR_KV + t) + 2)
                    by_token(kv_group(t), W_KV, t)
                elif t == T - 2:
                    pe.wait_ge(ut_ready, 2 * (TR_KV + T))
                    last_two(kv_group(t), W_KV)
                if t == 0:
                    normed(TR_KV, 1, T - 1)
                if t == 2:
                    build_row(FIRST["gm1"], 3)
                if t >= 1:
                    k_transposed(t - 1)
                    q_input(t - 1)
            for nh in range(2):
                for t in range(T):
                    pe.wait_ge(ut_ready, 2 * (TR_Q + t) + 2)
                    g = FIRST["q"] + T * nh + t
                    by_token(g, W_Q + 4 * nh, t)
                    if nh == 0 and t == 0:
                        k_transposed(T - 1)
                        q_input(T - 1)

            def side_turn(event):
                kind, pair = event
                if SIDE.index(event):
                    before, count = SIDE[SIDE.index(event) - 1]
                    pe.wait_ge(q_taken if before == "q" else at_ready, count + 1)
                if kind == "o":
                    pe.wait_ge(out_ready, 2 * pair + 2)
                for j in range(4):
                    last = pe.transpose(ps[:, X + 3, j * P:(j + 1) * P],
                                        resid[:, pair // 2, (4 * (pair % 2) + j) * P:(4 * (pair % 2) + j + 1) * P],
                                        ident[:])
                last.then_inc(side_t, 1)

            def side(n):
                if n % 2 == 1 and (n + 3) // 2 < UNITS // 2:
                    side_turn(("q", (n + 3) // 2))
                if n % 2 == 0 and n >= 4:
                    side_turn(("o", (n - 4) // 2))

            def make_scores(n):
                b, u = n // 4, n % 4
                lo = P if b == 0 else 0
                m, part = u // 2, slice(u % 2 * HD, (u % 2 + 1) * HD)
                pe.wait_ge(q_taken, n // 2 + 1)
                if n >= 2:
                    pe.wait_ge(max_ready, n - 1)
                for g in range(GROUP):
                    bank, at = 2 * (n % 2) + g // 2, g % 2 * 2 * P
                    last = pe.matmul(ps[:, bank, at + lo:at + 2 * P], acc[part, (4 * m + g) * P:(4 * m + g + 1) * P],
                                     kt[part, m, (b - 1) * P + lo:(b + 1) * P], start=True, stop=True)
                last.then_inc(scores, 1)

            def turn_p(n):
                pe.wait_ge(exp_ready, n + 1)
                if n:
                    pe.wait_ge(p_taken, n)
                for j in range(1 if n < 4 else 0, 2):
                    for g in range(GROUP):
                        last = pe.transpose(ps[:, X + j, g * P:(g + 1) * P],
                                            probs[:, n % 3, g, j * P:(j + 1) * P], ident[:])
                last.then_inc(p_t, 1)

            def make_pv(n):
                b, u = n // 4, n % 4
                pe.wait_ge(p_taken, n + 1)
                if n:
                    pe.wait_ge(out_ready, n)
                first = 1 if b == 0 else 0
                for g in range(GROUP):
                    for j in range(first, 2):
                        last = pe.matmul(ps[:, X + 2, g * HD:(g + 1) * HD], probst[:, n % 2, j, g * P:(g + 1) * P],
                                         vv[:, b - 1 + j, u * HD:(u + 1) * HD], start=(j == first), stop=(j == 1))
                last.then_inc(pv_done, 1)

            pe.wait_ge(roped, 3 * T)
            pe.wait_ge(kt_evac, T)
            pe.wait_ge(ut_ready, 2 * (TR_Q + T))
            side_turn(("q", 0))
            make_scores(0)
            make_scores(1)
            side_turn(("q", 1))
            for n in range(UNITS + 1):
                if n + 2 < UNITS:
                    make_scores(n + 2)
                if n < UNITS:
                    turn_p(n)
                side(n)
                if n:
                    make_pv(n - 1)
            side_turn(("o", UNITS // 2 - 1))
            pe.wait_ge(at_ready, 2 * T)
            for t in range(T):
                by_token(FIRST["op0"] + t, W_OP, t)
            second_half("op1", "gf1", 4, W_OP + 4, 2, TR_LN2)
            mlp_chunk(FIRST["mlp1"], W_MLP1, LOADS_MLP1, 8 * CHUNKS, head=lambda t: normed(TR_LN2, 2, t))
            with pe.Fori(1, end) as i:
                mlp_chunk(FIRST["mlp1"], W_MLP1, LOADS_MLP1, 8 * CHUNKS, i, 8)
            mlp_chunk(FIRST["mlp1"] + 24 * end, W_MLP1 + 8 * end, LOADS_MLP1 + 8 * end, 8 * CHUNKS + 8 * end)


def arrange(inputs):
    f = {k: np.asarray(a) for k, a in inputs.items()}
    ada = [f["ada_w"][0].reshape(K, P, 6, D), f["kv_ada_w"].reshape(K, P, 2, D), f["ada_w"][1].reshape(K, P, 6, D)]
    bias = [f["ada_b"][0].reshape(6, D), f["kv_ada_b"].reshape(2, D), f["ada_b"][1].reshape(6, D)]
    where = [(0, 1), (0, 0), (0, 2), (0, 3), (0, 4), (0, 5), (1, 0), (1, 1), (2, 0), (2, 1), (2, 2), (2, 3), (2, 4),
             (2, 5)]

    def by_feature(rows):
        return np.ascontiguousarray(np.stack(rows).reshape(len(rows), K, P).transpose(2, 0, 1))

    def up_blocks(w):
        n = w.shape[1] // P
        return w.reshape(K, P, n, P).transpose(2, 1, 0, 3).reshape(n, P, D)

    def half_blocks(w):
        n = w.shape[1] // HALF
        return w.reshape(4, 2, P, n, HALF).transpose(3, 0, 2, 1, 4).reshape(4 * n, P, D)

    a_in, nq = f["a_w_in"][0], H * P
    blocks = [up_blocks(a_in[:, 0:2 * nq]), half_blocks(a_in[:, 2 * nq:2 * nq + D]),
              half_blocks(a_in[:, 2 * nq + D:2 * nq + 2 * D]), half_blocks(f["a_w_out"][0])]
    w_q = f["b_w_q"][0].reshape(D, 2, 2, GROUP, HD).transpose(0, 1, 3, 2, 4).reshape(D, D)
    for layer in range(2):
        up, down = up_blocks(f["mlp_w_up"][layer]), f["mlp_w_down"][layer].reshape(DFF // P, P, D)
        blocks.append(np.stack([up.reshape(CHUNKS, 4, P, D), down.reshape(CHUNKS, 4, P, D)], 1).reshape(-1, P, D))
        if layer == 0:
            blocks += [half_blocks(f["w_kv"]), half_blocks(w_q), half_blocks(f["b_w_o"][0])]
    blocks = np.concatenate(blocks)
    stream = np.empty((N_LOADS, P, D), np.float32)
    for n, x in enumerate(ORDER):
        stream[n] = blocks[x[1]] if x[0] == "w" else ada[where[x[1]][0]][x[2], :, where[x[1]][1]]
    early = np.stack([ada[0][4 * half:4 * half + 4, :, which] for which in (1, 0) for half in range(2)])
    j = np.arange(2 * P)[None, :]
    i = np.arange(P)[:, None]
    return {
        "stream": stream,
        "early": np.ascontiguousarray(early.transpose(0, 2, 1, 3)).reshape(4, P, 4 * D),
        "xt": np.ascontiguousarray(f["x"][0].T).reshape(K, P, S),
        "x": np.ascontiguousarray(f["x"][0]),
        "pair_sum": np.tile(np.eye(8, dtype=np.float32), (2, 1)),
        "ident": np.eye(P, dtype=np.float32),
        "mod_bias": by_feature([bias[m][r] for m, r in where]),
        "fcols": by_feature([*f["ln_g"][0:3], *f["ln_b"][0:3], f["a_norm_w"][0]]),
        "c": np.ascontiguousarray(f["c"][0].reshape(K, P).T),
        "gate_w": np.ascontiguousarray(a_in[:, 2 * nq + 2 * D:].reshape(K, P, 8).transpose(1, 0, 2).reshape(P, K * 8)),
        "gate_b": np.repeat(f["a_b_gates"][0], T),
        "ln_g": np.ascontiguousarray(f["ln_g"]),
        "ln_b": np.ascontiguousarray(f["ln_b"]),
        "sinks": np.ascontiguousarray(f["b_sinks"][0]),
        "positions": np.ascontiguousarray(f["positions"][0].reshape(T, P).T),
        "inv_freq": (np.float32(THETA) ** (-np.arange(RH, dtype=np.float32) / np.float32(RH))).astype(np.float32),
        "mask": np.where((j > i) & (j <= i + P), 0.0, MASKED).astype(np.float32),
    }


def kernel(**inputs):
    import concourse.bacc as bacc
    from concourse.bass_utils import run_bass_kernel_spmd

    nc = bacc.Bacc("TRN2", target_bir_lowering=False, num_devices=1)
    arrays = {"in_" + k: a for k, a in arrange(inputs).items()}
    aps = {k[3:]: nc.dram_tensor(k, a.shape, mybir.dt.from_np(a.dtype), kind="ExternalInput").ap()
           for k, a in arrays.items()}
    out = nc.dram_tensor("out", (S, D), F32, kind="ExternalOutput").ap()
    build(nc, aps.pop("stream"), aps.pop("early"), aps.pop("xt"), aps.pop("x"), aps, out)
    result = run_bass_kernel_spmd(nc, [arrays], core_ids=[0])
    return result.results[0]["out"].reshape(1, S, D)
```
